# Optimizing a Trainium2 kernel written in Bass

```python
import math
import jax, jax.numpy as jnp
from jax import lax
import numpy as np

D_MODEL = 1024
BATCH = 1
SEQ = 256
DEPTH = 2

HEAD_DIM = 64
N_HEADS = D_MODEL // HEAD_DIM
N_KV_GROUPS = 2
HEADS_PER_GROUP = N_HEADS // N_KV_GROUPS
KV_DIM = N_KV_GROUPS * HEAD_DIM
CMP_BLOCK = 32
CMP_STRIDE = 16
CMP_HIDDEN = 256
SEL_BLOCK = 64
N_SELECT = 16
WINDOW = 512
Q_BLOCK = 128
SEL_FORCE = 100.0
ROPE_THETA = 10000.0
SCALE = HEAD_DIM ** -0.5
LRU_WIDTH = D_MODEL
LRU_HEADS = 16
LRU_BLOCK = LRU_WIDTH // LRU_HEADS
LRU_C = 8.0
CONV_WIDTH = 4
SSM_INNER = D_MODEL
SSM_HEAD_DIM = 64
SSM_HEADS = SSM_INNER // SSM_HEAD_DIM
SSM_GROUPS = 2
SSM_STATE = 128
SSM_CHUNK = 128
SSM_CONV_DIM = SSM_INNER + 2 * SSM_GROUPS * SSM_STATE
PEER_HEADS = 8
PEER_KEYS = 128
PEER_EXPERTS = PEER_KEYS * PEER_KEYS
PEER_QUERY_DIM = 256
PEER_HALF = PEER_QUERY_DIM // 2
PEER_TOPK = 16
PEER_CHUNK = 128
N_BRANCH = 3
IN_SIZES = (N_HEADS * HEAD_DIM, 6 * KV_DIM, 3 * N_HEADS,
            LRU_WIDTH, LRU_WIDTH,
            SSM_INNER, SSM_CONV_DIM, SSM_HEADS,
            N_BRANCH * D_MODEL)
IN_COLS = sum(IN_SIZES)
EPS = 1e-6
NEG = -1e30

kernel_name = 'hybrid_nsa_rglru_ssd_peer'

def rms_norm(x, g):
    x32 = x.astype(jnp.float32)
    y = x32 * lax.rsqrt(jnp.mean(x32 * x32, axis=-1, keepdims=True) + EPS)
    return (y * g.astype(jnp.float32)).astype(x.dtype)

def rope(x, positions):
    half = x.shape[-1] // 2
    inv = ROPE_THETA ** (-jnp.arange(half, dtype=jnp.float32) / half)
    ang = positions.astype(jnp.float32)[..., None] * inv
    cos = jnp.cos(ang)[:, :, None, :]
    sin = jnp.sin(ang)[:, :, None, :]
    x32 = x.astype(jnp.float32)
    x1, x2 = x32[..., :half], x32[..., half:]
    return jnp.concatenate([x1 * cos - x2 * sin, x2 * cos + x1 * sin], axis=-1).astype(x.dtype)

def masked_softmax(s, mask):
    s32 = jnp.where(mask, s.astype(jnp.float32), NEG)
    return jax.nn.softmax(s32, axis=-1) * mask

def causal_conv(x, w, b):
    k_w, s = w.shape[0], x.shape[1]
    xp = jnp.pad(x, ((0, 0), (k_w - 1, 0), (0, 0)))
    out = b
    for k in range(k_w):
        out = out + xp[:, k:k + s] * w[k]
    return out

def segsum(a):
    t = a.shape[-1]
    rep = jnp.broadcast_to(a[..., None], a.shape + (t,))
    strict = jnp.tril(jnp.ones((t, t), dtype=bool), -1)
    cs = jnp.cumsum(jnp.where(strict, rep, 0.0), axis=-2)
    return jnp.where(jnp.tril(jnp.ones((t, t), dtype=bool)), cs, -jnp.inf)

def linear_recurrence_combine(left, right):
    a1, b1 = left
    a2, b2 = right
    return a1 * a2, a2 * b1 + b2

def nsa_branch(q, kv, gate_logits, positions, q_norm_g, k_norm_g, cmp_pe_k, cmp_pe_v,
               cmp_k_w1, cmp_k_w2, cmp_v_w1, cmp_v_w2):
    B, S = q.shape[:2]
    G, HG, dh = N_KV_GROUPS, HEADS_PER_GROUP, HEAD_DIM
    q = rope(rms_norm(q.reshape(B, S, N_HEADS, dh), q_norm_g), positions)
    k_c, v_c, k_s, v_s, k_w, v_w = [a.reshape(B, S, G, dh) for a in jnp.split(kv, 6, axis=-1)]
    k_c = rope(rms_norm(k_c, k_norm_g), positions)
    k_s = rope(rms_norm(k_s, k_norm_g), positions)
    k_w = rope(rms_norm(k_w, k_norm_g), positions)
    gates = jax.nn.sigmoid(gate_logits).reshape(B, S, G, HG, 3)

    n_cmp = (S - CMP_BLOCK) // CMP_STRIDE + 1
    cmp_start = CMP_STRIDE * jnp.arange(n_cmp)
    cmp_idx = cmp_start[:, None] + jnp.arange(CMP_BLOCK)[None, :]

    def compress(t, pe, w1, w2):
        blk = t[:, cmp_idx] + pe[None, None, :, None, :]
        blk = blk.transpose(0, 1, 3, 2, 4).reshape(B, n_cmp, G, CMP_BLOCK * dh)
        return jax.nn.gelu(blk @ w1) @ w2

    k_cmp = rms_norm(compress(k_c, cmp_pe_k, cmp_k_w1, cmp_k_w2), k_norm_g)
    v_cmp = compress(v_c, cmp_pe_v, cmp_v_w1, cmp_v_w2)
    cmp_end = cmp_start + CMP_BLOCK - 1

    n_sel = S // SEL_BLOCK
    n_pick = min(N_SELECT, n_sel)
    sel_start = SEL_BLOCK * jnp.arange(n_sel)
    overlap = jnp.clip(jnp.minimum(cmp_start[:, None] + CMP_BLOCK, sel_start[None, :] + SEL_BLOCK)
                       - jnp.maximum(cmp_start[:, None], sel_start[None, :]), 0).astype(jnp.float32) / CMP_BLOCK
    ks_blk = k_s.reshape(B, n_sel, SEL_BLOCK, G, dh).transpose(0, 3, 1, 2, 4)
    vs_blk = v_s.reshape(B, n_sel, SEL_BLOCK, G, dh).transpose(0, 3, 1, 2, 4)
    b_ix = jnp.arange(B)[:, None, None, None]
    g_ix = jnp.arange(G)[None, :, None, None]
    blk_ids = jnp.arange(n_sel)

    kw_pad = jnp.pad(k_w, ((0, 0), (WINDOW, 0), (0, 0), (0, 0)))
    vw_pad = jnp.pad(v_w, ((0, 0), (WINDOW, 0), (0, 0), (0, 0)))

    n_qb = S // Q_BLOCK
    q_blocks = q.reshape(B, n_qb, Q_BLOCK, G, HG, dh).transpose(1, 0, 2, 3, 4, 5)
    g_blocks = gates.reshape(B, n_qb, Q_BLOCK, G, HG, 3).transpose(1, 0, 2, 3, 4, 5)

    def query_block(args):
        qb, gb, ib = args
        t = ib * Q_BLOCK + jnp.arange(Q_BLOCK)
        s_c = jnp.einsum('bqghd,bcgd->bghqc', qb, k_cmp) * SCALE
        p_c = masked_softmax(s_c, cmp_end[None, :] <= t[:, None])
        o_c = jnp.einsum('bghqc,bcgd->bqghd', p_c.astype(qb.dtype), v_cmp)
        imp = jnp.einsum('bghqc,cj->bgqj', p_c, overlap)
        cur = t // SEL_BLOCK
        causal_blk = sel_start[None, :] <= t[:, None]
        forced = (blk_ids[None, :] == 0) | (blk_ids[None, :] == cur[:, None]) | (blk_ids[None, :] == cur[:, None] - 1)
        score = jnp.where(forced, SEL_FORCE, jnp.where(causal_blk, imp, -1.0))
        _, sel = lax.top_k(score, n_pick)
        kg = ks_blk[b_ix, g_ix, sel]
        vg = vs_blk[b_ix, g_ix, sel]
        key_pos = sel[..., None] * SEL_BLOCK + jnp.arange(SEL_BLOCK)
        mask_s = (key_pos <= t[None, None, :, None, None]).reshape(B, G, 1, Q_BLOCK, n_pick * SEL_BLOCK)
        s_s = jnp.einsum('bqghd,bgqnld->bghqnl', qb, kg) * SCALE
        p_s = masked_softmax(s_s.reshape(B, G, HG, Q_BLOCK, n_pick * SEL_BLOCK), mask_s)
        p_s = p_s.reshape(B, G, HG, Q_BLOCK, n_pick, SEL_BLOCK).astype(qb.dtype)
        o_s = jnp.einsum('bghqnl,bgqnld->bqghd', p_s, vg)
        kw = lax.dynamic_slice_in_dim(kw_pad, ib * Q_BLOCK, Q_BLOCK + WINDOW, axis=1)
        vw = lax.dynamic_slice_in_dim(vw_pad, ib * Q_BLOCK, Q_BLOCK + WINDOW, axis=1)
        s_pos = ib * Q_BLOCK - WINDOW + jnp.arange(Q_BLOCK + WINDOW)
        mask_w = (s_pos[None, :] <= t[:, None]) & (s_pos[None, :] > t[:, None] - WINDOW) & (s_pos[None, :] >= 0)
        s_w = jnp.einsum('bqghd,bkgd->bghqk', qb, kw) * SCALE
        p_w = masked_softmax(s_w, mask_w)
        o_w = jnp.einsum('bghqk,bkgd->bqghd', p_w.astype(qb.dtype), vw)
        return gb[..., 0:1] * o_c + gb[..., 1:2] * o_s + gb[..., 2:3] * o_w

    out = lax.map(query_block, (q_blocks, g_blocks, jnp.arange(n_qb)))
    return out.transpose(1, 0, 2, 3, 4, 5).reshape(B, S, N_HEADS * dh)

def rglru_branch(x_in, gate_in, positions, conv_w, conv_b, w_r, b_r, w_i, b_i, lam):
    B, S, _ = x_in.shape
    xc = causal_conv(x_in, conv_w, conv_b)
    xh = xc.reshape(B, S, LRU_HEADS, LRU_BLOCK)
    r = jax.nn.sigmoid(jnp.einsum('bshi,hij->bshj', xh, w_r).reshape(B, S, LRU_WIDTH) + b_r)
    i = jax.nn.sigmoid(jnp.einsum('bshi,hij->bshj', xh, w_i).reshape(B, S, LRU_WIDTH) + b_i)
    log_a = -LRU_C * r.astype(jnp.float32) * jax.nn.softplus(-lam.astype(jnp.float32))
    reset = (positions == 0)[..., None]
    a = jnp.where(reset, 0.0, jnp.exp(log_a))
    mult = jnp.where(reset, 1.0, jnp.sqrt(-jnp.expm1(2.0 * log_a)))
    b = mult * (i * xc).astype(jnp.float32)
    _, h = lax.associative_scan(linear_recurrence_combine, (a, b), axis=1)
    return h.astype(x_in.dtype) * jax.nn.gelu(gate_in)

def ssd_chunked(x, dt, A, bm, cm):
    B, S = x.shape[:2]
    c, L = S // SSM_CHUNK, SSM_CHUNK
    G, HG, P, N = SSM_GROUPS, SSM_HEADS // SSM_GROUPS, SSM_HEAD_DIM, SSM_STATE
    X = (x.astype(jnp.float32) * dt[..., None]).reshape(B, c, L, G, HG, P)
    adt = (dt * A).reshape(B, c, L, G, HG).transpose(0, 3, 4, 1, 2)
    Bc = bm.astype(jnp.float32).reshape(B, c, L, G, N)
    Cc = cm.astype(jnp.float32).reshape(B, c, L, G, N)
    a_cs = jnp.cumsum(adt, axis=-1)
    decay = jnp.exp(segsum(adt))
    cb = jnp.einsum('bclgn,bcsgn->bgcls', Cc, Bc)
    y_diag = jnp.einsum('bghcls,bcsghp->bclghp', cb[:, :, None] * decay, X)
    decay_states = jnp.exp(a_cs[..., -1:] - a_cs).transpose(0, 3, 4, 1, 2)[..., None]
    states = jnp.einsum('bclgn,bclghp->bcghpn', Bc, X * decay_states)
    chunk_tot = jnp.pad(a_cs[..., -1], ((0, 0), (0, 0), (0, 0), (1, 0)))
    decay_chunk = jnp.exp(segsum(chunk_tot))
    states = jnp.concatenate([jnp.zeros_like(states[:, :1]), states], axis=1)
    states = jnp.einsum('bghzc,bcghpn->bzghpn', decay_chunk, states)[:, :-1]
    y_off = jnp.einsum('bclgn,bcghpn->bclghp', Cc, states) * jnp.exp(a_cs).transpose(0, 3, 4, 1, 2)[..., None]
    return (y_diag + y_off).reshape(B, S, SSM_HEADS, P).astype(x.dtype)

def ssd_branch(z, xbc, dt_raw, conv_w, conv_b, dt_bias, a_log, d_skip, norm_g):
    B, S, _ = z.shape
    xbc = jax.nn.silu(causal_conv(xbc, conv_w, conv_b))
    xs, bm, cm = jnp.split(xbc, [SSM_INNER, SSM_INNER + SSM_GROUPS * SSM_STATE], axis=-1)
    xs = xs.reshape(B, S, SSM_HEADS, SSM_HEAD_DIM)
    bm = bm.reshape(B, S, SSM_GROUPS, SSM_STATE)
    cm = cm.reshape(B, S, SSM_GROUPS, SSM_STATE)
    dt = jax.nn.softplus(dt_raw.astype(jnp.float32) + dt_bias.astype(jnp.float32))
    A = -jnp.exp(a_log.astype(jnp.float32))
    y = ssd_chunked(xs, dt, A, bm, cm) + d_skip[:, None] * xs
    y = y.reshape(B, S, SSM_INNER) * jax.nn.silu(z)
    y = rms_norm(y.reshape(B, S, SSM_GROUPS, SSM_INNER // SSM_GROUPS),
                 norm_g.reshape(SSM_GROUPS, SSM_INNER // SSM_GROUPS))
    return y.reshape(B, S, SSM_INNER)

def peer_ffn(h, w_q, sub_keys, u, v):
    B, S, D = h.shape
    n_ch = S // PEER_CHUNK
    hc = h.reshape(B, n_ch, PEER_CHUNK, D).transpose(1, 0, 2, 3)

    def chunk(hb):
        q = (hb @ w_q).reshape(B, PEER_CHUNK, PEER_HEADS, 2, PEER_HALF)
        s = jnp.einsum('bchxd,hxkd->bchxk', q, sub_keys).astype(jnp.float32)
        s1, i1 = lax.top_k(s[..., 0, :], PEER_TOPK)
        s2, i2 = lax.top_k(s[..., 1, :], PEER_TOPK)
        n_cand = PEER_TOPK * PEER_TOPK
        cand = (s1[..., :, None] + s2[..., None, :]).reshape(B, PEER_CHUNK, PEER_HEADS, n_cand)
        cidx = (i1[..., :, None] * PEER_KEYS + i2[..., None, :]).reshape(B, PEER_CHUNK, PEER_HEADS, n_cand)
        sc, pos = lax.top_k(cand, PEER_TOPK)
        eidx = jnp.take_along_axis(cidx, pos, axis=-1)
        g = jax.nn.softmax(sc, axis=-1)
        act = jax.nn.gelu(jnp.einsum('bchkd,bcd->bchk', u[eidx], hb).astype(jnp.float32))
        return jnp.einsum('bchk,bchkd->bcd', (g * act).astype(hb.dtype), v[eidx])

    out = lax.map(chunk, hc)
    return out.transpose(1, 0, 2, 3).reshape(B, S, D)

def hybrid_mixer(xn, positions, w_in, q_norm_g, k_norm_g, cmp_pe_k, cmp_pe_v, cmp_k_w1, cmp_k_w2,
                 cmp_v_w1, cmp_v_w2, lru_conv_w, lru_conv_b, lru_w_r, lru_b_r, lru_w_i, lru_b_i,
                 lru_lambda, ssm_conv_w, ssm_conv_b, ssm_dt_bias, ssm_a_log, ssm_d, ssm_norm_g,
                 w_branch, w_out):
    B, S, _ = xn.shape
    splits = np.cumsum(IN_SIZES)[:-1].tolist()
    a_q, a_kv, a_g, l_x, l_g, s_z, s_xbc, s_dt, m_g = [xn @ w for w in jnp.split(w_in, splits, axis=-1)]
    y_a = nsa_branch(a_q, a_kv, a_g, positions, q_norm_g, k_norm_g, cmp_pe_k, cmp_pe_v,
                     cmp_k_w1, cmp_k_w2, cmp_v_w1, cmp_v_w2)
    y_b = rglru_branch(l_x, l_g, positions, lru_conv_w, lru_conv_b, lru_w_r, lru_b_r,
                       lru_w_i, lru_b_i, lru_lambda)
    y_c = ssd_branch(s_z, s_xbc, s_dt, ssm_conv_w, ssm_conv_b, ssm_dt_bias, ssm_a_log, ssm_d, ssm_norm_g)
    merge_gates = jax.nn.sigmoid(m_g).reshape(B, S, N_BRANCH, D_MODEL)
    merged = (merge_gates[:, :, 0] * (y_a @ w_branch[0])
              + merge_gates[:, :, 1] * (y_b @ w_branch[1])
              + merge_gates[:, :, 2] * (y_c @ w_branch[2]))
    return merged @ w_out

def setup_inputs(seed: int = 0) -> dict:
    key = jax.random.key(seed)
    ks = jax.random.split(key, 32)
    f32 = jnp.float32
    L = DEPTH

    def nrm(k, shape, scale):
        return jax.random.normal(k, shape, f32) * scale

    def gain(k, shape):
        return 1.0 + 0.02 * jax.random.normal(k, shape, f32)

    u_lru = jax.random.uniform(ks[14], (L, LRU_WIDTH), f32, 0.9, 0.999)
    s_lru = u_lru ** (1.0 / LRU_C)
    dt0 = jnp.exp(jax.random.uniform(ks[17], (L, SSM_HEADS), f32, math.log(1e-3), math.log(1e-1)))
    return {
        'x': jax.random.normal(ks[0], (BATCH, SEQ, D_MODEL), f32),
        'positions': jnp.broadcast_to(jnp.arange(SEQ, dtype=jnp.int32)[None, :], (BATCH, SEQ)),
        'mix_norm_g': gain(ks[1], (L, D_MODEL)),
        'w_in': nrm(ks[2], (L, D_MODEL, IN_COLS), D_MODEL ** -0.5),
        'q_norm_g': gain(ks[3], (L, HEAD_DIM)),
        'k_norm_g': gain(ks[4], (L, HEAD_DIM)),
        'cmp_pe_k': nrm(ks[5], (L, CMP_BLOCK, HEAD_DIM), 0.1),
        'cmp_pe_v': nrm(ks[6], (L, CMP_BLOCK, HEAD_DIM), 0.1),
        'cmp_k_w1': nrm(ks[7], (L, CMP_BLOCK * HEAD_DIM, CMP_HIDDEN), (CMP_BLOCK * HEAD_DIM) ** -0.5),
        'cmp_k_w2': nrm(ks[8], (L, CMP_HIDDEN, HEAD_DIM), CMP_HIDDEN ** -0.5),
        'cmp_v_w1': nrm(ks[9], (L, CMP_BLOCK * HEAD_DIM, CMP_HIDDEN), (CMP_BLOCK * HEAD_DIM) ** -0.5),
        'cmp_v_w2': nrm(ks[10], (L, CMP_HIDDEN, HEAD_DIM), CMP_HIDDEN ** -0.5),
        'lru_conv_w': nrm(ks[11], (L, CONV_WIDTH, LRU_WIDTH), CONV_WIDTH ** -0.5),
        'lru_conv_b': nrm(ks[12], (L, LRU_WIDTH), 0.01),
        'lru_w_r': nrm(ks[13], (L, LRU_HEADS, LRU_BLOCK, LRU_BLOCK), LRU_BLOCK ** -0.5),
        'lru_b_r': nrm(ks[15], (L, LRU_WIDTH), 0.01),
        'lru_w_i': nrm(ks[16], (L, LRU_HEADS, LRU_BLOCK, LRU_BLOCK), LRU_BLOCK ** -0.5),
        'lru_b_i': nrm(ks[18], (L, LRU_WIDTH), 0.01),
        'lru_lambda': jnp.log(s_lru) - jnp.log1p(-s_lru),
        'ssm_conv_w': nrm(ks[19], (L, CONV_WIDTH, SSM_CONV_DIM), CONV_WIDTH ** -0.5),
        'ssm_conv_b': nrm(ks[20], (L, SSM_CONV_DIM), 0.01),
        'ssm_dt_bias': dt0 + jnp.log(-jnp.expm1(-dt0)),
        'ssm_a_log': jnp.log(jax.random.uniform(ks[21], (L, SSM_HEADS), f32, 1.0, 16.0)),
        'ssm_d': 1.0 + 0.1 * jax.random.normal(ks[22], (L, SSM_HEADS), f32),
        'ssm_norm_g': gain(ks[23], (L, SSM_INNER)),
        'w_branch': nrm(ks[24], (L, N_BRANCH, D_MODEL, D_MODEL), D_MODEL ** -0.5),
        'w_out': nrm(ks[25], (L, D_MODEL, D_MODEL), D_MODEL ** -0.5),
        'ffn_norm_g': gain(ks[26], (L, D_MODEL)),
        'peer_w_q': nrm(ks[27], (L, D_MODEL, PEER_HEADS * PEER_QUERY_DIM), D_MODEL ** -0.5),
        'peer_sub_keys': nrm(ks[28], (L, PEER_HEADS, 2, PEER_KEYS, PEER_HALF), PEER_HALF ** -0.5),
        'peer_u': nrm(ks[29], (L, PEER_EXPERTS, D_MODEL), D_MODEL ** -0.5),
        'peer_v': nrm(ks[30], (L, PEER_EXPERTS, D_MODEL), PEER_HEADS ** -0.5),
    }

def reference(x, positions, mix_norm_g, w_in, q_norm_g, k_norm_g, cmp_pe_k, cmp_pe_v, cmp_k_w1,
              cmp_k_w2, cmp_v_w1, cmp_v_w2, lru_conv_w, lru_conv_b, lru_w_r, lru_b_r, lru_w_i,
              lru_b_i, lru_lambda, ssm_conv_w, ssm_conv_b, ssm_dt_bias, ssm_a_log, ssm_d,
              ssm_norm_g, w_branch, w_out, ffn_norm_g, peer_w_q, peer_sub_keys, peer_u, peer_v):
    for l in range(DEPTH):
        xn = rms_norm(x, mix_norm_g[l])
        x = x + hybrid_mixer(xn, positions, w_in[l], q_norm_g[l], k_norm_g[l], cmp_pe_k[l], cmp_pe_v[l],
                             cmp_k_w1[l], cmp_k_w2[l], cmp_v_w1[l], cmp_v_w2[l], lru_conv_w[l],
                             lru_conv_b[l], lru_w_r[l], lru_b_r[l], lru_w_i[l], lru_b_i[l],
                             lru_lambda[l], ssm_conv_w[l], ssm_conv_b[l], ssm_dt_bias[l],
                             ssm_a_log[l], ssm_d[l], ssm_norm_g[l], w_branch[l], w_out[l])
        x = x + peer_ffn(rms_norm(x, ffn_norm_g[l]), peer_w_q[l], peer_sub_keys[l], peer_u[l], peer_v[l])
    return x


_drawn_inputs = setup_inputs


def setup_inputs(seed=0):
    import zlib

    import numpy as np

    out = dict(_drawn_inputs(seed))
    spreads = {}
    factors = {'q_norm_g': 3.937,
     'k_norm_g': 3.783,
     'cmp_pe_k': 2.928,
     'lru_b_r': 7.882,
     'lru_b_i': 7.115}
    for name, (base, spread) in spreads.items():
        noise = np.random.default_rng([zlib.crc32(name.encode()), seed]).standard_normal(out[name].shape)
        drawn = base * np.exp(spread * noise) if base else spread * noise
        out[name] = __import__('jax').numpy.asarray(drawn.astype(out[name].dtype))
    for name, factor in factors.items():
        out[name] = (out[name] * factor).astype(out[name].dtype)
    return out
```

```python
from contextlib import ExitStack

import numpy as np
import concourse.bass as bass
from concourse import mybir

ALU = mybir.AluOpType
ACT = mybir.ActivationFunctionType
F32 = mybir.dt.float32
I32 = mybir.dt.int32
U32 = mybir.dt.uint32
AX = mybir.AxisListType.X

P = 128
D = 1024
S = 256
L = 2
NT = S // P
KT = D // P
DH = 64
G = 2
NP = 8
NCMP = 15
CROWS = 31
EPS = 1e-6
SCALE = DH ** -0.5
NEG = -1e30
HALF = DH // 2
FX = 12
CONV = 4
PAD = CONV - 1
SH = 16
PH = 8
TOPK = 16
NKEY = 128
EXPERTS = NKEY * NKEY

KV0, KV1, Q0, LX0, LG0, XBC0, Z0 = 0, 1, 2, 4, 6, 8, 11
W1K, W1V, MG0 = 13, 14, 15
BR0, OUT0, PQ0 = 21, 27, 29
GROUPS = 33
KV1_COLS = 320
WCOL = 4096
RING = 3

KV_COLS = 832
VC, VS, VW, GATE, DTC = 384, 512, 640, 768, 816

_vec = {}
_at = 0
for _name, _n in (("mix_g", 8), ("conv_w", 32), ("conv_b", 8), ("b_r", 8), ("b_i", 8), ("lam", 8),
                  ("xconv_w", 48), ("xconv_b", 12), ("ssm_g", 8), ("pe", 32)):
    _vec[_name] = (_at, _at + _n)
    _at += _n
VEC = _at
LRU_W = 2 * KT * P
W2 = 2 * 2 * DH
SMALL = VEC + LRU_W + W2
ROW_DTB, ROW_ALOG, ROW_D, ROW_QG, ROW_KG, ROWS = 0, 16, 32, 48, 112, 176
C_ID, C_UP, C_STRICT, C_CAUSAL, C_CMPB, C_CMPM, C_INV, C_IOTA, CONSTS = (
    0, 128, 256, 384, 640, 672, 704, 736, 752)
TWO_PI = 2 * np.pi
PI_A = 6.28125
PI_B = float(np.float32(np.float32(round((TWO_PI - PI_A) * 2 ** 21)) / 2 ** 21))
PI_C = float(TWO_PI - PI_A - PI_B)
ROUND = 1.5 * 2 ** 23
SIN_MAX = 3.1415925
NU = 8
STEPS = PH * TOPK


def constants():
    c = np.zeros((P, CONSTS), np.float32)
    k, j = np.arange(P)[:, None], np.arange(P)[None, :]
    c[:, C_ID:C_ID + P] = k == j
    c[:, C_UP:C_UP + P] = k <= j
    c[:, C_STRICT:C_STRICT + P] = k > j
    c[:, C_CAUSAL + P:C_CAUSAL + 2 * P] = np.where(j > k, NEG, 0)
    for t in range(NT):
        end = 16 * np.arange(NCMP)[None, :] + 31
        ok = end <= k + t * P
        c[:, C_CMPB + 16 * t:C_CMPB + 16 * t + NCMP] = np.where(ok, 0, NEG)
        c[:, C_CMPM + 16 * t:C_CMPM + 16 * t + NCMP] = ok
    c[:, C_INV:C_INV + HALF] = np.float32(10000.0) ** (-np.arange(HALF, dtype=np.float32) / HALF)
    c[:, C_IOTA:C_IOTA + 16] = np.arange(16)
    return c


class Chain:

    def __init__(self, eng, sem):
        self.eng, self.sem, self.n = eng, sem, 0

    def add(self, ins):
        ins.then_inc(self.sem, 1)
        self.n += 1

    def settle(self):
        self.eng.wait_ge(self.sem, self.n)

    def link(self, ins):
        self.add(ins)
        self.settle()


def over(ap, n):
    return ap.unsqueeze(2).to_broadcast([ap.shape[0], ap.shape[1], n])


def times(ap, n):
    return ap.unsqueeze(1).to_broadcast([ap.shape[0], n, ap.shape[1]])


def trunk(nc, x_in, pos_tok, pos_row, const, wstream, small, rows, ffn_row, subkeys, table_u, table_v, out):
    V, A, PE, PO = nc.vector, nc.scalar, nc.tensor, nc.gpsimd
    with ExitStack() as ctx:
        def sb(name, shape, dt=F32, where=ctx):
            return where.enter_context(nc.sbuf_tensor(name, shape, dt))

        sems = {}

        def sem(name):
            sems[name] = ctx.enter_context(nc.semaphore(name))
            return sems[name]

        bank = [ctx.enter_context(nc.psum_tensor(f"bank{i}", [P, 512], F32)) for i in range(8)]

        cst = sb("cst", [P, CONSTS])
        ident = cst[:, C_ID:C_ID + P]
        upper = cst[:, C_UP:C_UP + P]
        strict = cst[:, C_STRICT:C_STRICT + P]
        x = sb("x", [P, NT, D])
        featT = sb("featT", [P, KT, S])
        rope_c = sb("rope_c", [P, NT, DH])
        rope_s = sb("rope_s", [P, NT, DH])
        not_reset = sb("not_reset", [P, S])
        is_reset = sb("is_reset", [P, S])
        row_base = sb("row_base", [P, 1])
        eps = sb("eps", [P, 1])
        st = sb("st", [P, 64])
        ring = sb("ring", [P, RING, WCOL])

        s_in = sem("inputs_loaded")
        s_setup = sem("setup")
        loaded = [sem(f"weights_loaded_{i}") for i in range(RING)]
        s_small = sem("small_loaded")
        s_rows = sem("rows_loaded")
        s_subk = sem("subkeys_loaded")
        s_dve, s_act, s_pool = sem("dve_chain"), sem("act_chain"), sem("pool_chain")
        s_proj, s_evac = sem("unit_multiplied"), sem("unit_taken")
        s_ssq, s_nrm, s_nt, s_ntev = sem("norm_root"), sem("x_normed"), sem("x_turned"), sem("xT_taken")
        s_kr, s_krt = sem("k_squares"), sem("k_root")
        s_qr, s_qrt = sem("q_squares"), sem("q_root")
        s_sp, s_spe = sem("softplus_in"), sem("softplus_exp")
        s_pads = sem("pads_zero")
        s_conv, s_lg, s_lgev = sem("lru_conv"), sem("lru_gate_multiplied"), sem("lru_gate_taken")
        s_la, s_lexp, s_lm, s_lsq = sem("lru_log_a"), sem("lru_exp"), sem("lru_one_minus_a2"), sem("lru_root")
        s_xconv, s_silu = sem("ssm_conv"), sem("ssm_silu")
        s_kvt, s_kvtev, s_qt, s_qtev = sem("kv_turned"), sem("kvT_taken"), sem("q_turned"), sem("qT_taken")
        s_ch, s_chg, s_cht, s_chtev = (sem("cmp_hidden"), sem("cmp_gelu"), sem("cmp_hidden_turned"),
                                       sem("cmp_hiddenT_taken"))
        s_co, s_cksq, s_ckrt, s_ckn = sem("cmp_out"), sem("cmp_k_squares"), sem("cmp_k_root"), sem("cmp_k_normed")
        s_ckt, s_cktev = sem("cmp_k_turned"), sem("cmp_kT_taken")
        s_cs, s_cmask, s_cexp, s_cp = (sem("cmp_scores"), sem("cmp_masked"), sem("cmp_exp"), sem("cmp_probs"))
        s_sig = sem("gates_sigmoid")
        s_sc, s_sctk, s_max, s_exp = sem("scores"), sem("scores_taken"), sem("row_max"), sem("row_exp")
        s_coef, s_scaled = sem("coefficients"), sem("probs_scaled")
        s_pt, s_ptev_a, s_ptev_v = sem("probs_turned"), sem("probsT_taken_act"), sem("probsT_taken_dve")
        s_y, s_yev = sem("attended"), sem("attended_taken")
        s_ea, s_adt, s_sd, s_sde = sem("exp_a"), sem("adt"), sem("ssd_sums"), sem("ssd_sums_exp")
        s_xt, s_xtev, s_xd = sem("xs_turned"), sem("xs_taken"), sem("x_times_dt")
        s_cb, s_cbm, s_au = sem("cb"), sem("cb_masked"), sem("adt_upper")
        s_seg, s_dec, s_m = sem("segsum"), sem("decay"), sem("cb_times_decay")
        s_yd, s_ydtk = sem("ssd_y"), sem("ssd_y_taken")
        s_s0, s_s0ev, s_yo, s_yotk = sem("state"), sem("state_taken"), sem("y_off"), sem("y_off_taken")
        s_zy, s_zrt, s_zn, s_zt, s_ztev = (sem("gated_y"), sem("gated_root"), sem("gated_normed"),
                                           sem("gated_turned"), sem("gatedT_taken"))
        s_mgs, s_mrg, s_xout = sem("merge_sigmoid"), sem("merged"), sem("x_mixed")
        s_hrow = sem("ffn_row_loaded")
        s_hrt, s_hn, s_ht, s_htev = sem("h_root"), sem("h_normed"), sem("h_turned"), sem("hT_taken")
        s_ps, s_psev = sem("key_scores"), sem("key_scores_taken")
        s_cand, s_gexp, s_idx = sem("candidates"), sem("expert_softmax_exp"), sem("expert_rows")
        s_u = [sem(f"u_row_{i}") for i in range(NU)]
        s_v = [sem(f"v_row_{i}") for i in range(NU)]
        s_dot, s_gelu, s_w, s_diag, s_vacc, s_xffn = (sem("u_dot"), sem("expert_gelu"), sem("expert_weight"),
                                                      sem("expert_diag"), sem("v_added"), sem("x_ffn"))
        s_store = sem("stored")

        with ExitStack() as tmp:
            pt = sb("pt", [P, NT], I32, tmp)
            ptf = sb("ptf", [P, NT], F32, tmp)
            pr = sb("pr", [P, S], I32, tmp)
            prf = sb("prf", [P, S], F32, tmp)
            ang = sb("ang", [P, NT, HALF], F32, tmp)
            turn = sb("turn", [P, 2, NT, HALF], F32, tmp)
            arg = sb("arg", [P, 2, NT, HALF], F32, tmp)
            trig = sb("trig", [P, 2, NT, HALF], F32, tmp)
            with nc.Block(no_gpsimd_drain=True) as block:
                @block.sync
                def _(sp):
                    sp.dma_start(cst[:], const).then_inc(s_in, 16)
                    sp.dma_start(pt[:], pos_tok).then_inc(s_in, 16)
                    sp.dma_start(pr[:], pos_row.partition_broadcast(P)).then_inc(s_in, 16)
                    sp.dma_start(x[:], x_in.rearrange("(t p) d -> p t d", p=P)).then_inc(s_in, 16)

                @block.vector
                def _(dve):
                    ch = Chain(dve, s_dve)
                    V.memset(row_base[:], 0.0)
                    V.memset(eps[:], EPS)
                    dve.wait_ge(s_in, 64)
                    V.tensor_copy(ptf[:], pt[:])
                    ch.link(V.tensor_copy(prf[:], pr[:]))
                    V.tensor_scalar(not_reset[:], prf[:], 0.0, None, ALU.not_equal)
                    V.tensor_scalar(is_reset[:], prf[:], 0.0, None, ALU.is_equal)
                    ch.link(V.tensor_tensor(ang[:], over(ptf[:], HALF),
                                            times(cst[:, C_INV:C_INV + HALF], NT), ALU.mult))
                    for j in range(2):
                        V.tensor_scalar(arg[:, j], ang[:], 1 / TWO_PI, 0.25 * j, ALU.mult, ALU.add).then_inc(s_dve, 1)
                        ch.n += 1
                    ch.settle()
                    ch.link(V.tensor_scalar(turn[:], arg[:], ROUND, None, ALU.add))
                    ch.link(V.tensor_scalar(turn[:], turn[:], -ROUND, None, ALU.add))
                    for j in range(2):
                        ch.add(V.scalar_tensor_tensor(arg[:, j], turn[:, j], -PI_A, ang[:], ALU.mult, ALU.add))
                    ch.settle()
                    ch.link(V.scalar_tensor_tensor(arg[:], turn[:], -PI_B, arg[:], ALU.mult, ALU.add))
                    ch.link(V.scalar_tensor_tensor(arg[:], turn[:], -PI_C, arg[:], ALU.mult, ALU.add))
                    ch.link(V.tensor_scalar(arg[:, 1], arg[:, 1], np.pi / 2, None, ALU.add))
                    V.tensor_scalar(arg[:], arg[:], SIN_MAX, -SIN_MAX, ALU.min, ALU.max).then_inc(s_setup, 1)
                    dve.wait_ge(s_setup, 2)
                    V.tensor_copy(rope_c[:, :, 0:HALF], trig[:, 1])
                    V.tensor_copy(rope_c[:, :, HALF:DH], trig[:, 1])
                    V.tensor_scalar(rope_s[:, :, 0:HALF], trig[:, 0], -1.0, None, ALU.mult)
                    V.tensor_copy(rope_s[:, :, HALF:DH], trig[:, 0]).then_inc(s_setup, 1)
                    dve.wait_ge(s_setup, 3)

                @block.scalar
                def _(act):
                    act.wait_ge(s_setup, 1)
                    A.activation(trig[:], arg[:], ACT.Sin).then_inc(s_setup, 1)

        all_sems = list(sems.values())
        first, last_sem = min(q.num for q in all_sems), max(q.num for q in all_sems)

        def clear():
            nc.gpsimd.dma_reset(range(first, last_sem + 1))
            nc.all_engine_barrier(sem_only=True)
            nc.sync.sem_clear(range(first, last_sem + 1))
            nc.all_engine_barrier(sem_only=True)

        clear()

        with nc.Fori(0, L) as layer:
            dch, ach, pch = Chain(V, s_dve), Chain(A, s_act), Chain(PO, s_pool)

            def load(sp, g):
                if g >= RING:
                    sp.wait_ge(s_proj, 2 * (g - RING + 1))
                w = ring[:, g % RING]
                src = wstream[bass.ds(layer * GROUPS + g, 1)].rearrange("a p c -> (a p) c")
                if g == KV1:
                    src, w = src[:, 0:KT * KV1_COLS], w[:, 0:KT * KV1_COLS]
                sp.dma_start(w, src).then_inc(loaded[g % RING], 16)

            def weights(g, cols=512):
                return ring[:, g % RING, 0:KT * cols].rearrange("p (k c) -> p k c", k=KT)

            def arrived(pe, g):
                pe.wait_ge(loaded[g % RING], 16 * (g // RING + 1))

            def token_unit(pe, g, t, src, nb, cols=512):
                u = 2 * g + t
                if t == 0:
                    arrived(pe, g)
                w = weights(g, cols)
                for k in range(KT):
                    mm = PE.matmul(bank[u % nb][:, 0:cols], src[:, k, t * P:(t + 1) * P], w[:, k, :],
                                   start=(k == 0), stop=(k == KT - 1))
                mm.then_inc(s_proj, 1)

            def feature_unit(pe, g, half, src, nb):
                u = 2 * g + half
                if half == 0:
                    arrived(pe, g)
                w = weights(g)
                for f in range(2):
                    for k in range(KT):
                        mm = PE.matmul(bank[u % nb][:, f * S:(f + 1) * S],
                                       w[:, k, (2 * half + f) * P:(2 * half + f + 1) * P], src[:, k, :],
                                       start=(k == 0), stop=(k == KT - 1))
                mm.then_inc(s_proj, 1)

            mix = ExitStack()
            with mix:
                tok_q = sb("tok_q", [P, NT, D], F32, mix)
                tok_kv = sb("tok_kv", [P, NT, KV_COLS], F32, mix)
                tok_z = sb("tok_z", [P, NT, D], F32, mix)
                lxT = sb("lxT", [P, KT, S + PAD], F32, mix)
                xbcT = sb("xbcT", [P, FX, S + PAD], F32, mix)
                xbcC = sb("xbcC", [P, FX, S], F32, mix)
                xcT = sb("xcT", [P, KT, S], F32, mix)
                lgT = sb("lgT", [P, KT, S], F32, mix)
                big = sb("big", [P, 3 * KT * S], F32, mix)
                smw = sb("smw", [P, SMALL], F32, mix)
                row = sb("row", [P, ROWS], F32, mix)
                sp_x = sb("sp_x", [P, 6, 40], F32, mix)
                expa = sb("expa", [P, SH], F32, mix)
                adt = sb("adt", [P, NT, SH], F32, mix)

                mgT = big[:].rearrange("p (f s) -> p f s", f=3 * KT)
                normed = big[:, 0:NT * D].rearrange("p (t d) -> p t d", t=NT)
                scr_a, scr_b = big[:, 2048:3072], big[:, 3072:4096]
                scr_act = big[:, 4096:5120]
                gate_r = big[:, 0:2048].rearrange("p (f s) -> p f s", f=KT)
                gate_i = big[:, 2048:4096].rearrange("p (f s) -> p f s", f=KT)
                lru_a = big[:, 4096:6144].rearrange("p (f s) -> p f s", f=KT)
                a_sq = lxT[:].rearrange("p f s -> p (f s)")[:, 0:KT * S].rearrange("p (f s) -> p f s", f=KT)
                sp_arg, sp_e, sp_w, sp_w2, sp_p, sp_out = (sp_x[:, j] for j in range(6))
                dt = sp_out[:, 0:2 * SH].rearrange("p (t h) -> p t h", t=NT)
                lru_c = sp_out[:, 32:40]

                def vec(name):
                    return smw[:, _vec[name][0]:_vec[name][1]]

                w_lru = smw[:, VEC:VEC + LRU_W].rearrange("p (j f c) -> p j f c", j=2, f=KT)
                w2 = smw[:, VEC + LRU_W:SMALL].rearrange("p (j k c) -> p j k c", j=2, k=2)

                NB = 4
                with nc.Block(no_gpsimd_drain=True) as block:
                    @block.sync
                    def _(sp):
                        sp.dma_start(smw[:], small[bass.ds(layer, 1)].rearrange("a p c -> (a p) c")).then_inc(s_small, 16)
                        sp.dma_start(row[:], rows[bass.ds(layer, 1)].rearrange("a c -> (a c)").partition_broadcast(P)
                                     ).then_inc(s_rows, 16)
                        for g in range(MG0 + 1):
                            load(sp, g)

                    @block.tensor
                    def _(pe):
                        for t in range(NT):
                            pe.wait_ge(s_nrm, t + 1)
                            for h in range(2):
                                if t:
                                    pe.wait_ge(s_ntev, h + 1)
                                for j in range(4):
                                    tr = PE.transpose(bank[6 + h][:, j * P:(j + 1) * P],
                                                      normed[:, t, (4 * h + j) * P:(4 * h + j + 1) * P], ident)
                                tr.then_inc(s_nt, 1)
                        pe.wait_ge(s_ntev, 4)

                        def free(u):
                            if u >= NB:
                                pe.wait_ge(s_evac, u - NB + 1)

                        for g in (KV0, KV1, Q0, Q0 + 1):
                            for t in range(NT):
                                free(2 * g + t)
                                token_unit(pe, g, t, featT, NB, KV1_COLS if g == KV1 else 512)
                        for g in range(LX0, XBC0 + 1):
                            for h in range(2):
                                free(2 * g + h)
                                feature_unit(pe, g, h, featT, NB)
                        pe.wait_ge(s_conv, 1)
                        for f in range(KT):
                            if f >= 2:
                                pe.wait_ge(s_lgev, f - 1)
                            for j in range(2):
                                mm = PE.matmul(bank[4 + f % 2][:, j * S:(j + 1) * S], w_lru[:, j, f, :], xcT[:, f, :],
                                               start=True, stop=True)
                            mm.then_inc(s_lg, 1)
                        for g in range(XBC0 + 1, Z0):
                            for h in range(2):
                                free(2 * g + h)
                                feature_unit(pe, g, h, featT, NB)
                        for g in (Z0, Z0 + 1):
                            for t in range(NT):
                                free(2 * g + t)
                                token_unit(pe, g, t, featT, NB)

                    @block.scalar
                    def _(act):
                        for t in range(NT):
                            ach.link(A.activation(scr_act[:], x[:, t, :], ACT.Square, accum_out=st[:, t:t + 1]))
                        A.activation(st[:, 2:4], st[:, 0:2], ACT.Sqrt, bias=eps[:], scale=1 / D).then_inc(s_ssq, 1)

                        def take(u, dst, func=ACT.Copy, cols=512):
                            act.wait_ge(s_proj, u + 1)
                            src = bank[u % NB][:, 0:cols]
                            if len(dst.shape) == 3:
                                src = src.rearrange("p (f s) -> p f s", f=2)
                            A.activation(dst, src, func).then_inc(s_evac, 1)

                        for t in range(NT):
                            take(2 * KV0 + t, tok_kv[:, t, 0:512])
                        for t in range(NT):
                            take(2 * KV1 + t, tok_kv[:, t, 512:KV_COLS], cols=KV1_COLS)
                        for t in range(NT):
                            act.wait_ge(s_kr, t + 1)
                            A.activation(st[:, 8 + 6 * t:14 + 6 * t], st[:, 8 + 6 * t:14 + 6 * t], ACT.Sqrt,
                                         scale=1 / DH).then_inc(s_krt, 1)
                        for g in range(2):
                            for t in range(NT):
                                take(2 * (Q0 + g) + t, tok_q[:, t, g * 512:(g + 1) * 512])
                        act.wait_ge(s_sp, 1)
                        A.activation(sp_e, sp_e, ACT.Exp).then_inc(s_spe, 1)
                        act.wait_ge(s_rows, 16)
                        A.activation(expa[:], row[:, ROW_ALOG:ROW_ALOG + SH], ACT.Exp).then_inc(s_ea, 1)
                        for t in range(NT):
                            act.wait_ge(s_qr, t + 1)
                            A.activation(st[:, 20 + 16 * t:36 + 16 * t], st[:, 20 + 16 * t:36 + 16 * t], ACT.Sqrt,
                                         scale=1 / DH).then_inc(s_qrt, 1)
                        act.wait_ge(s_pads, 2)
                        for n in range(4):
                            take(2 * LX0 + n, lxT[:, 2 * n:2 * n + 2, PAD:])
                        for n in range(4):
                            take(2 * LG0 + n, lgT[:, 2 * n:2 * n + 2, :], ACT.Gelu_apprx_tanh)
                        for n in range(2):
                            take(2 * XBC0 + n, xbcT[:, 2 * n:2 * n + 2, PAD:])
                        for f in range(KT):
                            act.wait_ge(s_lg, f + 1)
                            A.activation(gate_r[:, f, :], bank[4 + f % 2][:, 0:S], ACT.Sigmoid,
                                         bias=vec("b_r")[:, f:f + 1])
                            A.activation(gate_i[:, f, :], bank[4 + f % 2][:, S:2 * S], ACT.Sigmoid,
                                         bias=vec("b_i")[:, f:f + 1]).then_inc(s_lgev, 1)
                        for n in range(2, 6):
                            take(2 * XBC0 + n, xbcT[:, 2 * n:2 * n + 2, PAD:])
                        act.wait_ge(s_la, 1)
                        A.activation(lru_a[:], gate_r[:], ACT.Exp, scale=-1.0).then_inc(s_lexp, 1)
                        A.activation(gate_r[:], gate_r[:], ACT.Tanh).then_inc(s_lexp, 1)
                        act.wait_ge(s_lm, 1)
                        A.activation(gate_r[:], gate_r[:], ACT.Sqrt).then_inc(s_lsq, 1)
                        for g in range(2):
                            for t in range(NT):
                                take(2 * (Z0 + g) + t, tok_z[:, t, g * 512:(g + 1) * 512], ACT.Silu)
                        act.wait_ge(s_xconv, 1)
                        for n in range(3):
                            A.activation(xbcC[:, 4 * n:4 * n + 4, :], xbcC[:, 4 * n:4 * n + 4, :], ACT.Silu).then_inc(s_silu, 1)
                        act.wait_ge(s_silu, 3)

                    @block.vector
                    def _(dve):
                        V.memset(lxT[:, :, 0:PAD], 0.0).then_inc(s_pads, 1)
                        V.memset(xbcT[:, :, 0:PAD], 0.0).then_inc(s_pads, 1)
                        dve.wait_ge(s_ssq, 1)
                        dch.link(V.reciprocal(st[:, 4:6], st[:, 2:4]))
                        for t in range(NT):
                            V.tensor_scalar(normed[:, t, :], x[:, t, :], st[:, 4 + t:5 + t], None, ALU.mult).then_inc(s_nrm, 1)
                        dve.wait_ge(s_small, 16)
                        dve.wait_ge(s_rows, 16)
                        for t in range(NT):
                            for h in range(2):
                                dve.wait_ge(s_nt, 2 * t + h + 1)
                                V.tensor_tensor(featT[:, 4 * h:4 * h + 4, t * P:(t + 1) * P],
                                                bank[6 + h][:].rearrange("p (f s) -> p f s", f=4),
                                                over(vec("mix_g")[:, 4 * h:4 * h + 4], P), ALU.mult).then_inc(s_ntev, 1)

                        def head_norm_rope(src, nh, at, gain, squares, root, t):
                            v = src.rearrange("p (h d) -> p h d", h=nh)
                            a = scr_a[:, 0:nh * DH].rearrange("p (h d) -> p h d", h=nh)
                            b = scr_b[:, 0:nh * DH].rearrange("p (h d) -> p h d", h=nh)
                            ss = st[:, at:at + nh]
                            dch.link(V.tensor_tensor(a, v, v, ALU.mult))
                            dch.link(V.tensor_reduce(ss, a, AX, ALU.add))
                            V.tensor_scalar(ss, ss, DH * EPS, None, ALU.add).then_inc(squares, 1)
                            dve.wait_ge(root, t + 1)
                            dch.link(V.reciprocal(ss, ss))
                            dch.link(V.tensor_tensor(v, v, over(ss, DH), ALU.mult))
                            dch.link(V.tensor_tensor(v, v, times(gain, nh), ALU.mult))
                            dch.add(V.tensor_tensor(a, v, times(rope_c[:, t, :], nh), ALU.mult))
                            dch.add(V.tensor_tensor(b[:, :, 0:HALF], v[:, :, HALF:DH],
                                                    times(rope_s[:, t, 0:HALF], nh), ALU.mult))
                            dch.link(V.tensor_tensor(b[:, :, HALF:DH], v[:, :, 0:HALF],
                                                     times(rope_s[:, t, HALF:DH], nh), ALU.mult))
                            dch.link(V.tensor_tensor(v, a, b, ALU.add))

                        dve.wait_ge(s_evac, 4)
                        for t in range(NT):
                            dch.add(V.tensor_tensor(sp_arg[:, t * SH:(t + 1) * SH], tok_kv[:, t, DTC:DTC + SH],
                                                    row[:, ROW_DTB:ROW_DTB + SH], ALU.add))
                        dch.link(V.tensor_scalar(sp_arg[:, 32:40], vec("lam"), -1.0, None, ALU.mult))
                        dch.link(V.scalar_tensor_tensor(sp_e, sp_arg, -1.0, sp_arg, ALU.mult, ALU.min))
                        V.tensor_scalar(sp_out, sp_arg, 0.0, None, ALU.max).then_inc(s_sp, 1)
                        for t in range(NT):
                            head_norm_rope(tok_kv[:, t, 0:384], 6, 8 + 6 * t, row[:, ROW_KG:ROW_KG + DH], s_kr, s_krt, t)
                        dve.wait_ge(s_spe, 1)
                        dch.link(V.tensor_scalar(sp_w, sp_e, 2.0, None, ALU.add))
                        dch.link(V.reciprocal(sp_w, sp_w))
                        dch.link(V.tensor_tensor(sp_w, sp_w, sp_e, ALU.mult))
                        dch.link(V.tensor_tensor(sp_w2, sp_w, sp_w, ALU.mult))
                        dch.link(V.tensor_scalar(sp_p, sp_w2, 1 / 15, None, ALU.mult))
                        for n in (13, 11, 9, 7, 5, 3):
                            dch.link(V.scalar_tensor_tensor(sp_p, sp_p, 1 / n, sp_w2, ALU.add, ALU.mult))
                        dch.link(V.scalar_tensor_tensor(sp_p, sp_p, 1.0, sp_w, ALU.add, ALU.mult))
                        dch.link(V.scalar_tensor_tensor(sp_out, sp_p, 2.0, sp_out, ALU.mult, ALU.add))
                        dch.add(V.tensor_scalar(lru_c, lru_c, 8.0, None, ALU.mult))
                        dve.wait_ge(s_ea, 1)
                        dch.add(V.scalar_tensor_tensor(adt[:], dt, -1.0, times(expa[:], NT), ALU.mult, ALU.mult))
                        dve.wait_ge(s_evac, 8)
                        for t in range(NT):
                            head_norm_rope(tok_q[:, t, :], 16, 20 + 16 * t, row[:, ROW_QG:ROW_QG + DH], s_qr, s_qrt, t)

                        def conv(dst, src, n, w, b):
                            for k in range(CONV):
                                for f in range(n):
                                    wk = w[:, k * n + f:k * n + f + 1]
                                    if k == 0:
                                        ins = V.tensor_scalar(dst[:, f, :], src[:, f, 0:S], wk, b[:, f:f + 1], ALU.mult, ALU.add)
                                    else:
                                        ins = V.scalar_tensor_tensor(dst[:, f, :], src[:, f, k:k + S], wk, dst[:, f, :],
                                                                     ALU.mult, ALU.add)
                                    dch.add(ins)
                                dch.settle()

                        dve.wait_ge(s_evac, 12)
                        conv(xcT, lxT, KT, vec("conv_w"), vec("conv_b"))
                        dve.sem_inc(s_conv, 1)
                        dve.wait_ge(s_lgev, KT)
                        V.tensor_tensor(gate_r[:], gate_r[:], over(lru_c, S), ALU.mult).then_inc(s_la, 1)
                        dch.link(V.tensor_tensor(gate_i[:], gate_i[:], xcT[:], ALU.mult))
                        dve.wait_ge(s_lexp, 2)
                        dch.link(V.tensor_tensor(a_sq, lru_a[:], lru_a[:], ALU.mult))
                        dch.link(V.scalar_tensor_tensor(gate_r[:], a_sq, 1.0, gate_r[:], ALU.add, ALU.mult))
                        V.tensor_scalar(gate_r[:], gate_r[:], 1e-30, None, ALU.max).then_inc(s_lm, 1)
                        dch.link(V.tensor_tensor(lru_a[:], lru_a[:], times(not_reset[:], KT), ALU.mult))
                        dve.wait_ge(s_evac, 22)
                        conv(xbcC, xbcT, FX, vec("xconv_w"), vec("xconv_b"))
                        dve.sem_inc(s_xconv, 1)
                        dve.wait_ge(s_lsq, 1)
                        dch.link(V.tensor_tensor(gate_r[:], gate_r[:], times(not_reset[:], KT), ALU.mult))
                        dch.link(V.tensor_tensor(gate_r[:], gate_r[:], times(is_reset[:], KT), ALU.add))
                        dch.link(V.tensor_tensor(gate_i[:], gate_i[:], gate_r[:], ALU.mult))
                        for f in range(KT):
                            dch.add(V.tensor_tensor_scan(xcT[:, f, :], lru_a[:, f, :], gate_i[:, f, :], 0.0,
                                                         ALU.mult, ALU.add))
                        dch.settle()
                        dve.wait_ge(s_evac, 16)
                        dch.link(V.tensor_tensor(lgT[:], lgT[:], xcT[:], ALU.mult))

                mid = ExitStack()
                with mid:
                    qT = sb("qT", [P, NP, S], F32, mid)
                    kT = sb("kT", [P, 2, S], F32, mid)
                    scratch = sb("scratch", [P, 4352], F32, mid)
                    vcmp = sb("vcmp", [NCMP, 2 * DH], F32, mid)
                    kcmpT = sb("kcmpT", [P, NCMP], F32, mid)
                    gsig = sb("gsig", [P, NT, 48], F32, mid)
                    rst = sb("rst", [P, 2, 3, 4], F32, mid)
                    cst2 = sb("cst2", [P, 3, SH], F32, mid)
                    ssd_e = sb("ssd_e", [P, NT, 2 * SH], F32, mid)
                    kst = sb("kst", [NCMP, 4], F32, mid)

                    yaT = tok_q[:].rearrange("p t d -> p (t d)").rearrange("p (f s) -> p f s", f=KT)
                    ycT = qT
                    sc = scratch[:, 0:2048].rearrange("p (b j k) -> p b j k", b=2, j=4)
                    pT = scratch[:, 2048:4096].rearrange("p (b k c) -> p b k c", b=2, k=2)
                    lx_free = lxT[:].rearrange("p f s -> p (f s)")
                    pc = lx_free[:, 0:256].rearrange("p (h c) -> p h c", h=16)
                    pcT = lx_free[0:NCMP, 256:768].rearrange("p (b c) -> p b c", b=2)
                    cT = lx_free[:, 0:1024].rearrange("p (j g s) -> p j g s", j=2, g=G)
                    blocks = lx_free[:, 0:1024].rearrange("p (j s) -> p j s", j=2)
                    chid = lx_free[0:CROWS, 1024:1536]
                    chT = lx_free[:, 1536:1536 + 4 * CROWS].rearrange("p (j c) -> p j c", j=4)
                    ck = lx_free[0:NCMP, 1664:1792]
                    cksq = lx_free[0:NCMP, 1792:1920]
                    xs_tok = xcT[:].rearrange("p f s -> p (f s)").rearrange("p (t d) -> p t d", t=NT)
                    flat = xbcT[:].rearrange("p f s -> p (f s)")
                    xdt = flat[:, 0:2048].rearrange("p (t d) -> p t d", t=NT)
                    xdec = flat[:, 2048:3072]
                    b_tok = scratch[:, 0:256].rearrange("p (g n) -> p g n", g=G)
                    cbm = scratch[:, 256:768].rearrange("p (c g l) -> p c g l", c=NT, g=G)
                    au = scratch[:, 768:1792].rearrange("p (b h l) -> p b h l", b=2, h=4)
                    dec = scratch[:, 1792:2816].rearrange("p (b h l) -> p b h l", b=2, h=4)
                    s0 = scratch[:, 2816:3840].rearrange("p (g c) -> p g c", g=G)
                    yt = scratch[:, 3840:4352]
                    yt2 = lx_free[:, 0:512]
                    zsq = lx_free[:, 512:1024]
                    units = [(t, i) for t in range(NT) for i in range(NP)]
                    MGU = 2 * MG0
                    NMG = 12

                    with nc.Block(no_gpsimd_drain=True) as block:
                        @block.sync
                        def _(sp):
                            for g in range(MG0 + 1, BR0 + 2):
                                load(sp, g)

                        @block.tensor
                        def _(pe):
                            def gates(n):
                                if n < NMG:
                                    u = MGU + n
                                    if n >= 2:
                                        pe.wait_ge(s_evac, 26 + n - 1)
                                    feature_unit(pe, u // 2, u % 2, featT, 2)

                            for t in range(NT):
                                for j, c in enumerate((0, 128, 256, VC)):
                                    tr = PE.transpose(bank[2 + t][:, j * P:(j + 1) * P], tok_kv[:, t, c:c + P], ident)
                                tr.then_inc(s_kvt, 1)
                            for n in range(4):
                                t, h = n // 2, n % 2
                                if n >= 2:
                                    pe.wait_ge(s_qtev, n - 1)
                                for j in range(4):
                                    c = (4 * h + j) * P
                                    tr = PE.transpose(bank[4 + h][:, j * P:(j + 1) * P], tok_q[:, t, c:c + P], ident)
                                tr.then_inc(s_qt, 1)
                            pe.wait_ge(s_kvtev, 2)
                            for j, g in enumerate((W1K, W1V)):
                                arrived(pe, g)
                                w1 = ring[:, g % RING].rearrange("p (l c) -> p l c", l=16)
                                o = bank[7][0:CROWS, j * S:(j + 1) * S]
                                pe_col = vec("pe")
                                for q in range(16):
                                    PE.matmul(o, blocks[:, j, 2 * q:2 * q + 16 * (CROWS - 1) + 1:16], w1[:, q, :],
                                              start=(q == 0), stop=False)
                                    mm = PE.matmul(o, pe_col[:, 16 * j + q:16 * j + q + 1].to_broadcast([P, CROWS]), w1[:, q, :],
                                                   start=False, stop=(q == 15))
                                mm.then_inc(s_proj, 2)
                            PE.matmul(bank[6][0:1, 0:1], ident[:, 0:1], ident[:, 0:1], start=True, stop=True).then_inc(s_ch, 1)
                            gates(0)
                            pe.wait_ge(s_chg, 1)
                            for j in range(4):
                                tr = PE.transpose(bank[7][:, j * CROWS:(j + 1) * CROWS], chid[:, j * P:(j + 1) * P], ident[0:CROWS, 0:CROWS])
                            tr.then_inc(s_cht, 1)
                            gates(1)
                            pe.wait_ge(s_chtev, 1)
                            for j in range(2):
                                for g in range(G):
                                    for k in range(2):
                                        mm = PE.matmul(bank[6][0:NCMP, (2 * j + g) * DH:(2 * j + g + 1) * DH],
                                                       chT[:, 2 * j + k, g * 16:g * 16 + NCMP], w2[:, j, k, :],
                                                       start=(k == 0), stop=(k == 1))
                            mm.then_inc(s_co, 1)
                            gates(2)
                            pe.wait_ge(s_ckn, 1)
                            PE.transpose(bank[7][:, 0:NCMP], ck[:], ident[0:NCMP, 0:NCMP]).then_inc(s_ckt, 1)
                            pe.wait_ge(s_qtev, 4)
                            pe.wait_ge(s_cktev, 1)

                            def cmp_scores(t):
                                if t:
                                    pe.wait_ge(s_sctk, 2 * NP)
                                    pe.wait_ge(s_yev, 2)
                                for i in range(NP):
                                    for g in range(G):
                                        mm = PE.matmul(bank[2 + g][:, i * 16:i * 16 + NCMP], qT[g * DH:(g + 1) * DH, i, t * P:(t + 1) * P],
                                                       kcmpT[g * DH:(g + 1) * DH, :], start=True, stop=True)
                                mm.then_inc(s_cs, 1)

                            def scores(n):
                                t, i = units[n]
                                nk = (t + 1) * P
                                if i == 0:
                                    pe.wait_ge(s_cmask, 2 * t + 2)
                                elif n:
                                    pe.wait_ge(s_sctk, 2 * n)
                                for g in range(G):
                                    for b in range(2):
                                        mm = PE.matmul(bank[2 + g][:, b * nk:(b + 1) * nk],
                                                       qT[g * DH:(g + 1) * DH, i, t * P:(t + 1) * P],
                                                       kT[g * DH:(g + 1) * DH, b, 0:nk], start=True, stop=True)
                                mm.then_inc(s_sc, 1)

                            def turn(n):
                                t, i = units[n]
                                pe.wait_ge(s_scaled, n + 1)
                                pe.wait_ge(s_cp, t + 1)
                                if n:
                                    pe.wait_ge(s_ptev_a, 2 * n)
                                if n > NP:
                                    pe.wait_ge(s_ptev_v, n - NP)
                                for k in range(t + 1):
                                    for j in range(4):
                                        PE.transpose(bank[4 + k][:, j * P:(j + 1) * P], sc[:, n % 2, j, k * P:(k + 1) * P], ident)
                                for g in range(G):
                                    tr = PE.transpose(bank[7][0:NCMP, g * P:(g + 1) * P], pc[:, 2 * i + g, 0:NCMP], ident)
                                tr.then_inc(s_pt, 1)

                            def attend(n):
                                t, i = units[n]
                                pe.wait_ge(s_ptev_a, 2 * (n + 1))
                                if t:
                                    pe.wait_ge(s_ptev_v, n - NP + 1)
                                if n % 4 == 0 and n:
                                    pe.wait_ge(s_yev, n // 4)
                                for g in range(G):
                                    o = bank[6][g * DH:(g + 1) * DH, (n % 4) * P:(n % 4 + 1) * P]
                                    first_one = True
                                    for b, c in enumerate((VS, VW)):
                                        for k in range(t + 1):
                                            PE.matmul(o, tok_kv[:, k, c + g * DH:c + (g + 1) * DH],
                                                      pT[:, n % 2, k, (2 * g + b) * P:(2 * g + b + 1) * P],
                                                      start=first_one, stop=False)
                                            first_one = False
                                    mm = PE.matmul(o, vcmp[:, g * DH:(g + 1) * DH], pcT[:, n % 2, g * P:(g + 1) * P],
                                                   start=False, stop=True)
                                mm.then_inc(s_y, 1)

                            for n in range(len(units) + 1):
                                if n == 0:
                                    cmp_scores(0)
                                if n < len(units):
                                    if n == NP:
                                        turn(n - 1)
                                        gates(n + 2)
                                        attend(n - 1)
                                        cmp_scores(1)
                                        scores(n)
                                        continue
                                    scores(n)
                                if n:
                                    turn(n - 1)
                                    gates(n + 2)
                                    attend(n - 1)

                            pe.wait_ge(s_yev, 4)
                            for c in range(NT):
                                PE.matmul(bank[7][:, 2 * c * SH:(2 * c + 1) * SH], upper, adt[:, c, :], start=True, stop=True)
                                mm = PE.matmul(bank[7][:, (2 * c + 1) * SH:(2 * c + 2) * SH], strict, adt[:, c, :],
                                               start=True, stop=True)
                            mm.then_inc(s_sd, 1)
                            for n in range(4):
                                c, h = n // 2, n % 2
                                if n >= 2:
                                    pe.wait_ge(s_xtev, n - 1)
                                for j in range(4):
                                    tr = PE.transpose(bank[4 + h][:, j * P:(j + 1) * P],
                                                      xbcC[:, 4 * h + j, c * P:(c + 1) * P], ident)
                                tr.then_inc(s_xt, 1)
                            for g in range(G):
                                tr = PE.transpose(bank[6][:, g * P:(g + 1) * P], xbcC[:, 8 + g, 0:P], ident)
                            tr.then_inc(s_xt, 1)
                            pe.wait_ge(s_sde, 1)
                            for c in range(NT):
                                for g in range(G):
                                    mm = PE.matmul(bank[7][:, (2 * c + g) * P:(2 * c + g + 1) * P],
                                                   xbcC[:, 8 + g, c * P:(c + 1) * P], xbcC[:, 10 + g, c * P:(c + 1) * P],
                                                   start=True, stop=True)
                            mm.then_inc(s_cb, 1)
                            pe.wait_ge(s_xd, 2)
                            pe.wait_ge(s_xtev, 5)
                            for g in range(G):
                                PE.matmul(bank[g][:], b_tok[:, g, :], xdec[:, g * 512:(g + 1) * 512],
                                          start=True, stop=True).then_inc(s_s0, 1)

                            def segsum(n):
                                pe.wait_ge(s_au, n + 1)
                                if n >= 2:
                                    pe.wait_ge(s_dec, n - 1)
                                PE.matmul(bank[2 + n % 2][:], strict, au[:, n % 2].rearrange("p h l -> p (h l)"),
                                          start=True, stop=True).then_inc(s_seg, 1)

                            def ssd_y(n):
                                c, q = n // 4, n % 4
                                g = q // 2
                                pe.wait_ge(s_m, n + 1)
                                if q % 2 == 0 and 2 * c + g >= 2:
                                    pe.wait_ge(s_ydtk, 2 * c + g - 1)
                                for j in range(4):
                                    h = 4 * q + j
                                    mm = PE.matmul(bank[4 + g][:, (h % 8) * DH:(h % 8 + 1) * DH], dec[:, n % 2, j, :],
                                                   xdt[:, c, h * DH:(h + 1) * DH], start=True, stop=True)
                                mm.then_inc(s_yd, 1)

                            for n in range(9):
                                if n < 8:
                                    segsum(n)
                                if n:
                                    ssd_y(n - 1)
                            pe.wait_ge(s_s0ev, 2)
                            for g in range(G):
                                PE.matmul(bank[g][:], xbcC[:, 10 + g, P:S], s0[:, g, :], start=True, stop=True).then_inc(s_yo, 1)
                            for n in range(4):
                                t, h = n // 2, n % 2
                                pe.wait_ge(s_zn, n + 1)
                                if n >= 2:
                                    pe.wait_ge(s_ztev, n - 1)
                                for j in range(4):
                                    tr = PE.transpose(bank[6 + h][:, j * P:(j + 1) * P],
                                                      tok_z[:, t, (4 * h + j) * P:(4 * h + j + 1) * P], ident)
                                tr.then_inc(s_zt, 1)

                        @block.scalar
                        def _(act):
                            def take_gates(n):
                                if n < NMG:
                                    act.wait_ge(s_proj, MGU + n + 1)
                                    A.activation(mgT[:, 2 * n:2 * n + 2, :],
                                                 bank[n % 2][:].rearrange("p (f s) -> p f s", f=2), ACT.Copy).then_inc(s_evac, 1)

                            A.activation(gsig[:], tok_kv[:, :, GATE:GATE + 48], ACT.Sigmoid).then_inc(s_sig, 1)
                            for t in range(NT):
                                act.wait_ge(s_kvt, t + 1)
                                for j, c in enumerate((0, 3)):
                                    for g in range(G):
                                        src = bank[2 + t][g * DH:(g + 1) * DH, c * P:(c + 1) * P]
                                        A.activation(cT[0:DH, j, g, t * P:(t + 1) * P], src, ACT.Copy)
                                        if t == 0:
                                            A.activation(cT[DH:P, j, g, 0:P - 1], src[:, 1:P], ACT.Copy)
                                        else:
                                            A.activation(cT[DH:P, j, g, P - 1:S - 1], src, ACT.Copy)
                                A.activation(kT[:, :, t * P:(t + 1) * P],
                                             bank[2 + t][:, P:3 * P].rearrange("p (b s) -> p b s", b=2),
                                             ACT.Copy).then_inc(s_kvtev, 1)
                            act.wait_ge(s_ch, 1)
                            A.activation(chid[:], bank[7][0:CROWS, :], ACT.Gelu_apprx_tanh).then_inc(s_chg, 1)
                            take_gates(0)
                            act.wait_ge(s_cht, 1)
                            A.activation(chT[:], bank[7][:, 0:4 * CROWS].rearrange("p (j c) -> p j c", j=4), ACT.Copy).then_inc(s_chtev, 1)
                            take_gates(1)
                            act.wait_ge(s_cksq, 1)
                            A.activation(kst[:, 0:2], kst[:, 0:2], ACT.Sqrt, scale=1 / DH).then_inc(s_ckrt, 1)
                            take_gates(2)
                            act.wait_ge(s_ckt, 1)
                            A.activation(kcmpT[:], bank[7][:, 0:NCMP], ACT.Copy).then_inc(s_cktev, 1)

                            def exps(n):
                                t, i = units[n]
                                nk = (t + 1) * P
                                act.wait_ge(s_max, n + 1)
                                for j in range(4):
                                    e = A.activation(sc[:, n % 2, j, 0:nk], sc[:, n % 2, j, 0:nk], ACT.Exp,
                                                     bias=rst[:, n % 2, 0, j:j + 1], accum_out=rst[:, n % 2, 1, j:j + 1])
                                e.then_inc(s_exp, 1)

                            def take_turned(n):
                                act.wait_ge(s_pt, n + 1)
                                if n >= 2:
                                    act.wait_ge(s_y, n - 1)
                                A.activation(pT[:, n % 2, 0, :], bank[4][:], ACT.Copy).then_inc(s_ptev_a, 1)
                                A.activation(pcT[:, n % 2, :], bank[7][0:NCMP, 0:2 * P], ACT.Copy).then_inc(s_ptev_a, 1)

                            def cmp_exp(t):
                                act.wait_ge(s_cand, t + 1)
                                A.activation(pc[:, :, 0:NCMP], pc[:, :, 0:NCMP], ACT.Exp).then_inc(s_cexp, 1)

                            for n in range(len(units) + 1):
                                if n == 0:
                                    cmp_exp(0)
                                if n == NP:
                                    take_turned(n - 1)
                                    take_gates(n + 2)
                                    cmp_exp(1)
                                    exps(n)
                                    continue
                                if n < len(units):
                                    exps(n)
                                if n:
                                    take_turned(n - 1)
                                    take_gates(n + 2)

                            act.wait_ge(s_sd, 1)
                            A.activation(ssd_e[:], bank[7][:, 0:4 * SH].rearrange("p (c h) -> p c h", c=NT), ACT.Exp).then_inc(s_sde, 1)
                            for n in range(4):
                                c, h = n // 2, n % 2
                                act.wait_ge(s_xt, n + 1)
                                A.activation(xs_tok[:, c, h * 512:(h + 1) * 512], bank[4 + h][:], ACT.Copy).then_inc(s_xtev, 1)
                            act.wait_ge(s_xt, 5)
                            A.activation(b_tok[:], bank[6][:, 0:2 * P].rearrange("p (g n) -> p g n", g=G), ACT.Copy).then_inc(s_xtev, 1)
                            for g in range(G):
                                act.wait_ge(s_s0, g + 1)
                                A.activation(s0[:, g, :], bank[g][:], ACT.Copy).then_inc(s_s0ev, 1)
                            for n in range(8):
                                act.wait_ge(s_seg, n + 1)
                                if n >= 2:
                                    act.wait_ge(s_yd, n - 1)
                                A.activation(dec[:, n % 2].rearrange("p h l -> p (h l)"), bank[2 + n % 2][:], ACT.Exp).then_inc(s_dec, 1)
                            for n in range(4):
                                t, h = n // 2, n % 2
                                act.wait_ge(s_zy, n + 1)
                                ach.link(A.activation(zsq[:], tok_z[:, t, h * 512:(h + 1) * 512], ACT.Square,
                                                      accum_out=st[:, 8 + n:9 + n]))
                                A.activation(st[:, 12 + n:13 + n], st[:, 8 + n:9 + n], ACT.Sqrt, bias=eps[:],
                                             scale=2 / D).then_inc(s_zrt, 1)
                            for b in range(3):
                                A.activation(mgT[:, 8 * b:8 * b + 8, :], mgT[:, 8 * b:8 * b + 8, :], ACT.Sigmoid).then_inc(s_mgs, 1)
                            act.wait_ge(s_mgs, 3)

                        @block.gpsimd
                        def _(pool):
                            for n in range(len(units)):
                                t, i = units[n]
                                nk = (t + 1) * P
                                pool.wait_ge(s_coef, n + 1)
                                PO.tensor_tensor(sc[:, n % 2, :, 0:nk], sc[:, n % 2, :, 0:nk],
                                                 over(rst[:, n % 2, 2, :], nk), ALU.mult).then_inc(s_scaled, 1)
                            for n in range(8):
                                c, q = n // 4, n % 4
                                if n >= 2:
                                    pool.wait_ge(s_seg, n - 1)
                                else:
                                    pool.wait_ge(s_pt, len(units))
                                PO.tensor_tensor(au[:, n % 2], times(upper, 4), over(adt[:, c, 4 * q:4 * q + 4], P),
                                                 ALU.mult).then_inc(s_au, 1)

                        @block.vector
                        def _(dve):
                            for n in range(4):
                                t, h = n // 2, n % 2
                                dve.wait_ge(s_qt, n + 1)
                                V.tensor_copy(qT[:, 4 * h:4 * h + 4, t * P:(t + 1) * P],
                                              bank[4 + h][:].rearrange("p (f s) -> p f s", f=4)).then_inc(s_qtev, 1)
                            dve.wait_ge(s_co, 1)
                            dch.add(V.tensor_copy(vcmp[:], bank[6][0:NCMP, P:2 * P]))
                            dch.link(V.tensor_copy(ck[:], bank[6][0:NCMP, 0:P]))
                            ckv = ck.rearrange("p (g d) -> p g d", g=G)
                            sqv = cksq.rearrange("p (g d) -> p g d", g=G)
                            dch.link(V.tensor_tensor(cksq[:], ck[:], ck[:], ALU.mult))
                            dch.link(V.tensor_reduce(kst[:, 0:2], sqv, AX, ALU.add))
                            V.tensor_scalar(kst[:, 0:2], kst[:, 0:2], DH * EPS, None, ALU.add).then_inc(s_cksq, 1)
                            dve.wait_ge(s_ckrt, 1)
                            dch.link(V.reciprocal(kst[:, 2:4], kst[:, 0:2]))
                            dch.link(V.tensor_tensor(ckv, ckv, over(kst[:, 2:4], DH), ALU.mult))
                            V.tensor_tensor(ckv, ckv, times(row[0:NCMP, ROW_KG:ROW_KG + DH], G), ALU.mult).then_inc(s_ckn, 1)

                            pcv = pc[:, :, 0:NCMP]

                            def cmp_max(t):
                                dve.wait_ge(s_cs, t + 1)
                                if t:
                                    dve.wait_ge(s_pt, NP)
                                pg = pc.rearrange("p (i g) c -> p i g c", g=G)
                                for g in range(G):
                                    V.scalar_tensor_tensor(pg[:, :, g, 0:NCMP],
                                                           bank[2 + g][:, 0:P].rearrange("p (i c) -> p i c", i=NP)[:, :, 0:NCMP],
                                                           SCALE, times(cst[:, C_CMPB + 16 * t:C_CMPB + 16 * t + NCMP], NP),
                                                           ALU.mult, ALU.add).then_inc(s_cmask, 1)
                                dve.wait_ge(s_cmask, 2 * t + 2)
                                dch.link(V.tensor_reduce(cst2[:, 0, :], pcv, AX, ALU.max))
                                V.tensor_tensor(pcv, pcv, over(cst2[:, 0, :], NCMP), ALU.subtract).then_inc(s_cand, 1)

                            def cmp_probs(t):
                                dve.wait_ge(s_cexp, t + 1)
                                dch.link(V.tensor_reduce(cst2[:, 1, :], pcv, AX, ALU.add))
                                dch.link(V.reciprocal(cst2[:, 1, :], cst2[:, 1, :]))
                                dch.link(V.tensor_tensor(cst2[:, 2, :], cst2[:, 1, :],
                                                         gsig[:, t, :].rearrange("p (h b) -> p h b", b=3)[:, :, 0], ALU.mult))
                                dch.link(V.tensor_tensor(pcv, pcv, over(cst2[:, 2, :], NCMP), ALU.mult))
                                V.tensor_tensor(pcv, pcv, times(cst[:, C_CMPM + 16 * t:C_CMPM + 16 * t + NCMP], 2 * NP),
                                                ALU.mult).then_inc(s_cp, 1)

                            def row_max(n):
                                t, i = units[n]
                                nk = (t + 1) * P
                                dve.wait_ge(s_sc, n + 1)
                                if n >= 2:
                                    dve.wait_ge(s_pt, n - 1)
                                mask = cst[:, C_CAUSAL + P:C_CAUSAL + 2 * P] if t == 0 else cst[:, C_CAUSAL:C_CAUSAL + 2 * P]
                                for g in range(G):
                                    V.scalar_tensor_tensor(sc[:, n % 2, 2 * g:2 * g + 2, 0:nk],
                                                           bank[2 + g][:, 0:2 * nk].rearrange("p (b k) -> p b k", b=2),
                                                           SCALE, times(mask, 2), ALU.mult, ALU.add).then_inc(s_sctk, 1)
                                dve.wait_ge(s_sctk, 2 * n + 2)
                                V.tensor_reduce(rst[:, n % 2, 0, :], sc[:, n % 2, :, 0:nk], AX, ALU.max,
                                                negate=True).then_inc(s_max, 1)

                            def coefficients(n):
                                t, i = units[n]
                                dve.wait_ge(s_exp, n + 1)
                                dch.link(V.reciprocal(rst[:, n % 2, 1, :], rst[:, n % 2, 1, :]))
                                V.tensor_tensor(rst[:, n % 2, 2, :].rearrange("p (g b) -> p g b", g=G),
                                                rst[:, n % 2, 1, :].rearrange("p (g b) -> p g b", g=G),
                                                gsig[:, t, :].rearrange("p (h b) -> p h b", b=3)[:, 2 * i:2 * i + 2, 1:3],
                                                ALU.mult).then_inc(s_coef, 1)

                            def take_turned(n):
                                t, i = units[n]
                                if t:
                                    dve.wait_ge(s_pt, n + 1)
                                    dve.wait_ge(s_y, n - 1)
                                    V.tensor_copy(pT[:, n % 2, 1, :], bank[5][:]).then_inc(s_ptev_v, 1)

                            def take_y(n):
                                if n % 4 == 3:
                                    t, q = n // 8, (n // 4) % 2
                                    dve.wait_ge(s_y, n + 1)
                                    V.tensor_copy(yaT[:, 4 * q:4 * q + 4, t * P:(t + 1) * P],
                                                  bank[6][:].rearrange("p (i s) -> p i s", i=4)).then_inc(s_yev, 1)

                            dve.wait_ge(s_sig, 1)
                            for n in range(len(units) + 1):
                                if n == 0:
                                    cmp_max(0)
                                    cmp_probs(0)
                                if n == NP:
                                    coefficients(n - 1)
                                    take_turned(n - 1)
                                    take_y(n - 1)
                                    cmp_max(1)
                                    cmp_probs(1)
                                    row_max(n)
                                    continue
                                if n < len(units):
                                    row_max(n)
                                if n:
                                    coefficients(n - 1)
                                    take_turned(n - 1)
                                    take_y(n - 1)

                            dve.wait_ge(s_xtev, 4)
                            dve.wait_ge(s_sde, 1)
                            xh = [xs_tok[:, c, :].rearrange("p (h d) -> p h d", h=SH) for c in range(NT)]
                            for c in range(NT):
                                dch.add(V.tensor_tensor(xdt[:, c, :].rearrange("p (h d) -> p h d", h=SH), xh[c],
                                                        over(dt[:, c, :], DH), ALU.mult))
                            dch.settle()
                            dve.sem_inc(s_xd, 1)
                            V.tensor_tensor(xdec.rearrange("p (h d) -> p h d", h=SH),
                                            xdt[:, 0, :].rearrange("p (h d) -> p h d", h=SH),
                                            over(ssd_e[:, 0, SH:2 * SH], DH), ALU.mult).then_inc(s_xd, 1)
                            dve.wait_ge(s_cb, 1)
                            dch.link(V.tensor_tensor(cbm.rearrange("p c g l -> p (c g) l"),
                                                     bank[7][:].rearrange("p (n l) -> p n l", n=4), times(upper, 4), ALU.mult))

                            def decayed(n):
                                c, q = n // 4, n % 4
                                dve.wait_ge(s_dec, n + 1)
                                V.tensor_tensor(dec[:, n % 2], dec[:, n % 2], times(cbm[:, c, q // 2, :], 4), ALU.mult).then_inc(s_m, 1)

                            def gated(c, g):
                                n = 2 * c + g
                                yh = yt.rearrange("p (h d) -> p h d", h=8)
                                dch.link(V.tensor_tensor(yh, xh[c][:, 8 * g:8 * g + 8, :],
                                                         over(row[:, ROW_D + 8 * g:ROW_D + 8 * g + 8], DH), ALU.mult))
                                dve.wait_ge(s_yd, 4 * c + 2 * g + 2)
                                V.tensor_tensor(yt, yt, bank[4 + g][:], ALU.add).then_inc(s_ydtk, 1)
                                dve.wait_ge(s_ydtk, n + 1)
                                if c:
                                    dve.wait_ge(s_yo, g + 1)
                                    dch.link(V.tensor_tensor(yt2.rearrange("p (h d) -> p h d", h=8),
                                                             bank[g][:].rearrange("p (h d) -> p h d", h=8),
                                                             over(ssd_e[:, 1, 8 * g:8 * g + 8], DH), ALU.mult))
                                    dch.link(V.tensor_tensor(yt, yt, yt2, ALU.add))
                                z = tok_z[:, c, g * 512:(g + 1) * 512]
                                V.tensor_tensor(z, z, yt, ALU.mult).then_inc(s_zy, 1)
                                dve.wait_ge(s_zy, n + 1)

                            def normed_z(n):
                                t, h = n // 2, n % 2
                                dve.wait_ge(s_zrt, n + 1)
                                dch.link(V.reciprocal(st[:, 16 + n:17 + n], st[:, 12 + n:13 + n]))
                                z = tok_z[:, t, h * 512:(h + 1) * 512]
                                V.tensor_scalar(z, z, st[:, 16 + n:17 + n], None, ALU.mult).then_inc(s_zn, 1)

                            for n in range(4):
                                decayed(n)
                            gated(0, 0)
                            gated(0, 1)
                            for n in range(4, 8):
                                decayed(n)
                            gated(1, 0)
                            gated(1, 1)
                            for n in range(4):
                                normed_z(n)
                            for n in range(4):
                                t, h = n // 2, n % 2
                                dve.wait_ge(s_zt, n + 1)
                                V.tensor_tensor(ycT[:, 4 * h:4 * h + 4, t * P:(t + 1) * P],
                                                bank[6 + h][:].rearrange("p (f s) -> p f s", f=4),
                                                over(vec("ssm_g")[:, 4 * h:4 * h + 4], P), ALU.mult).then_inc(s_ztev, 1)
                            dve.wait_ge(s_ztev, 4)

                    BU = 2 * BR0
                    EV0 = 26 + NMG
                    OU = 2 * OUT0
                    mtmp = scratch[:, 0:1024].rearrange("p (b c) -> p b c", b=2)
                    with nc.Block(no_gpsimd_drain=True) as block:
                        @block.sync
                        def _(sp):
                            for g in range(BR0 + 2, PQ0 + 2):
                                load(sp, g)

                        @block.tensor
                        def _(pe):
                            for n in range(12):
                                if n >= 4:
                                    pe.wait_ge(s_evac, EV0 + n - 3)
                                u = BU + n
                                feature_unit(pe, u // 2, u % 2, (yaT, lgT, ycT)[n // 4], 4)
                            pe.wait_ge(s_mrg, 1)
                            for n in range(4):
                                pe.wait_ge(s_evac, EV0 + 12 + n - 3)
                                u = OU + n
                                token_unit(pe, u // 2, u % 2, featT, 4)

                        @block.vector
                        def _(dve):
                            for n in range(12):
                                b, q = n // 4, n % 4
                                dve.wait_ge(s_proj, BU + n + 1)
                                src = bank[(BU + n) % 4][:].rearrange("p (f s) -> p f s", f=2)
                                gate = mgT[:, 8 * b + 2 * q:8 * b + 2 * q + 2, :]
                                dst = featT[:, 2 * q:2 * q + 2, :]
                                if b == 0:
                                    V.tensor_tensor(dst, src, gate, ALU.mult).then_inc(s_evac, 1)
                                    continue
                                mt = mtmp[:, n % 2].rearrange("p (f s) -> p f s", f=2)
                                V.tensor_tensor(mt, src, gate, ALU.mult).then_inc(s_evac, 1)
                                dve.wait_ge(s_evac, EV0 + n + 1)
                                dch.link(V.tensor_tensor(dst, dst, mt, ALU.add))
                            dve.sem_inc(s_mrg, 1)
                            for n in range(4):
                                t, h = n % 2, n // 2
                                dve.wait_ge(s_proj, OU + n + 1)
                                xv = x[:, t, h * 512:(h + 1) * 512]
                                V.tensor_tensor(xv, xv, bank[(OU + n) % 4][:], ALU.add).then_inc(s_evac, 1)
                            dve.wait_ge(s_evac, EV0 + 16)

            ffn = ExitStack()
            with ffn:
                h_tok = sb("h_tok", [P, NT, D], F32, ffn)
                s_key = sb("s_key", [P, NT, 16, P], F32, ffn)
                subk = sb("subk", [P, 16, P], F32, ffn)
                QU = 2 * PQ0
                EV1 = 26 + 12 + 16
                with ExitStack() as tmp:
                    qpT = sb("qpT", [P, 16, S], F32, tmp)
                    g_row = sb("g_row", [P, D], F32, tmp)
                    sq = sb("sq", [P, D], F32, tmp)
                    with nc.Block(no_gpsimd_drain=True) as block:
                        @block.sync
                        def _(sp):
                            sp.dma_start(g_row[:], ffn_row[bass.ds(layer, 1)].rearrange("a c -> (a c)").partition_broadcast(P)
                                         ).then_inc(s_hrow, 16)
                            sp.dma_start(subk[:], subkeys[bass.ds(layer, 1)].rearrange("a p c k -> (a p) c k")
                                         ).then_inc(s_subk, 16)
                            for g in range(PQ0 + 2, GROUPS):
                                load(sp, g)

                        @block.scalar
                        def _(act):
                            for t in range(NT):
                                ach.link(A.activation(sq[:], x[:, t, :], ACT.Square, accum_out=st[:, t:t + 1]))
                            A.activation(st[:, 2:4], st[:, 0:2], ACT.Sqrt, bias=eps[:], scale=1 / D).then_inc(s_hrt, 1)
                            for n in range(8):
                                act.wait_ge(s_proj, QU + n + 1)
                                A.activation(qpT[:, 2 * n:2 * n + 2, :],
                                             bank[(QU + n) % 4][:].rearrange("p (f s) -> p f s", f=2), ACT.Copy).then_inc(s_evac, 1)
                            for n in range(8):
                                act.wait_ge(s_ps, n + 1)
                                A.activation(s_key[:, n // 4, 4 * (n % 4):4 * (n % 4) + 4, :],
                                             bank[4 + n % 2][:].rearrange("p (f s) -> p f s", f=4), ACT.Copy).then_inc(s_psev, 1)
                            act.wait_ge(s_psev, 8)

                        @block.vector
                        def _(dve):
                            dve.wait_ge(s_hrt, 1)
                            dve.wait_ge(s_hrow, 16)
                            dch.link(V.reciprocal(st[:, 4:6], st[:, 2:4]))
                            for t in range(NT):
                                V.scalar_tensor_tensor(h_tok[:, t, :], x[:, t, :], st[:, 4 + t:5 + t], g_row[:],
                                                       ALU.mult, ALU.mult).then_inc(s_hn, 1)
                            for n in range(4):
                                t, h = n // 2, n % 2
                                dve.wait_ge(s_ht, n + 1)
                                V.tensor_copy(featT[:, 4 * h:4 * h + 4, t * P:(t + 1) * P],
                                              bank[6 + h][:].rearrange("p (f s) -> p f s", f=4)).then_inc(s_htev, 1)

                        @block.tensor
                        def _(pe):
                            for n in range(4):
                                t, h = n // 2, n % 2
                                pe.wait_ge(s_hn, t + 1)
                                if n >= 2:
                                    pe.wait_ge(s_htev, n - 1)
                                for j in range(4):
                                    tr = PE.transpose(bank[6 + h][:, j * P:(j + 1) * P],
                                                      h_tok[:, t, (4 * h + j) * P:(4 * h + j + 1) * P], ident)
                                tr.then_inc(s_ht, 1)
                            pe.wait_ge(s_htev, 4)
                            for n in range(8):
                                if n >= 4:
                                    pe.wait_ge(s_evac, EV1 + n - 3)
                                u = QU + n
                                feature_unit(pe, u // 2, u % 2, featT, 4)
                            pe.wait_ge(s_subk, 16)
                            pe.wait_ge(s_evac, EV1 + 8)
                            for n in range(8):
                                t = n // 4
                                if n >= 2:
                                    pe.wait_ge(s_psev, n - 1)
                                for j in range(4):
                                    hx = 4 * (n % 4) + j
                                    mm = PE.matmul(bank[4 + n % 2][:, j * P:(j + 1) * P], qpT[:, hx, t * P:(t + 1) * P],
                                                   subk[:, hx, :], start=True, stop=True)
                                mm.then_inc(s_ps, 1)

                with ExitStack() as tmp:
                    top_v = sb("top_v", [P, 16, TOPK], F32, tmp)
                    top_iu = sb("top_iu", [P, 16, TOPK], U32, tmp)
                    top_i = sb("top_i", [P, 16, TOPK], F32, tmp)
                    cut = sb("cut", [P, 256], F32, tmp)
                    cand = sb("cand", [P, PH, 256], F32, tmp)
                    hot = sb("hot", [P, PH * TOPK, 16], F32, tmp)
                    best = sb("best", [P, PH, TOPK], F32, tmp)
                    pos = sb("pos", [P, PH, TOPK], U32, tmp)
                    part = sb("part", [P, PH * TOPK], U32, tmp)
                    partf = sb("partf", [P, PH * TOPK], F32, tmp)
                    sel = sb("sel", [P, 2, PH * TOPK], F32, tmp)
                    rowf = sb("rowf", [P, PH * TOPK], F32, tmp)
                    rowi = sb("rowi", [P, NT, PH * TOPK], I32, tmp)
                    gw = sb("gw", [P, NT, PH, TOPK], F32, tmp)
                    gs = sb("gs", [P, 2, PH], F32, tmp)
                    ub = sb("ub", [P, NU, D], F32, tmp)
                    vb = sb("vb", [P, NU, D], F32, tmp)
                    dots = sb("dots", [P, NT, STEPS], F32, tmp)
                    diag = sb("diag", [P, 4, P], F32, tmp)
                    HEADS = NT * PH
                    ALL = NT * STEPS

                    with nc.Block(no_gpsimd_drain=True) as block:
                        @block.gpsimd
                        def _(pool):
                            for n in range(ALL + TOPK):
                                if n < ALL:
                                    t, j = divmod(n, STEPS)
                                    if j == 0:
                                        pool.wait_ge(s_idx, t + 1)
                                    if n >= NU:
                                        pool.wait_ge(s_dot, n - NU + 1)
                                    PO.indirect_dma_start(ub[:, n % NU, :], None, table_u,
                                                          bass.IndirectOffsetOnAxis(ap=rowi[:, t, j:j + 1], axis=0)
                                                          ).then_inc(s_u[n % NU], 16)
                                m = n - TOPK
                                if m >= 0:
                                    t, j = divmod(m, STEPS)
                                    if m >= NU:
                                        pool.wait_ge(s_vacc, m - NU + 1)
                                    PO.indirect_dma_start(vb[:, m % NU, :], None, table_v,
                                                          bass.IndirectOffsetOnAxis(ap=rowi[:, t, j:j + 1], axis=0)
                                                          ).then_inc(s_v[m % NU], 16)
                            for i in range(NU):
                                pool.wait_ge(s_u[i], 16 * (ALL // NU))
                                pool.wait_ge(s_v[i], 16 * (ALL // NU))

                        @block.vector
                        def _(dve):
                            def key_top(t, hx):
                                s = s_key[:, t, hx, :]
                                c = cut[:, 0:P]
                                dch.link(V.max(top_v[:, hx, 0:8], s))
                                dch.add(V.max_index(top_iu[:, hx, 0:8], top_v[:, hx, 0:8], s))
                                dch.link(V.match_replace(c, top_v[:, hx, 0:8], s, -3e38))
                                dch.link(V.max(top_v[:, hx, 8:16], c))
                                dch.add(V.max_index(top_iu[:, hx, 8:16], top_v[:, hx, 8:16], c))

                            def candidates(t):
                                dch.settle()
                                dch.add(V.tensor_copy(top_i[:], top_iu[:]))
                                tv = top_v[:].rearrange("p (h x) k -> p h x k", x=2)
                                for h in range(PH):
                                    dch.add(V.tensor_tensor(cand[:, h, :].rearrange("p (a b) -> p a b", a=TOPK),
                                                            over(tv[:, h, 0, :], TOPK), times(tv[:, h, 1, :], TOPK), ALU.add))
                                dch.settle()

                            def pair_top(h):
                                s = cand[:, h, :]
                                dch.link(V.max(best[:, h, 0:8], s))
                                dch.add(V.max_index(pos[:, h, 0:8], best[:, h, 0:8], s))
                                dch.link(V.match_replace(cut[:], best[:, h, 0:8], s, -3e38))
                                dch.link(V.max(best[:, h, 8:16], cut[:]))
                                dch.add(V.max_index(pos[:, h, 8:16], best[:, h, 8:16], cut[:]))

                            def experts(t):
                                dch.settle()
                                V.tensor_tensor(gw[:, t], best[:], over(best[:, :, 0], TOPK), ALU.subtract).then_inc(s_cand, 1)
                                pf = pos[:].rearrange("p h k -> p (h k)")
                                ti = top_i[:].rearrange("p (h x) k -> p h x k", x=2)
                                for half in range(2):
                                    dch.link(V.tensor_scalar(part[:], pf, (4, 15)[half], None,
                                                             (ALU.logical_shift_right, ALU.bitwise_and)[half]))
                                    dch.link(V.tensor_copy(partf[:], part[:]))
                                    dch.link(V.tensor_tensor(hot[:], over(partf[:], 16), times(cst[:, C_IOTA:C_IOTA + 16], STEPS),
                                                             ALU.is_equal))
                                    for h in range(PH):
                                        hh = hot[:, h * TOPK:(h + 1) * TOPK, :]
                                        dch.add(V.tensor_tensor(hh, hh, times(ti[:, h, half, :], TOPK), ALU.mult))
                                    dch.settle()
                                    dch.link(V.tensor_reduce(sel[:, half, :], hot[:], AX, ALU.add))
                                dch.link(V.scalar_tensor_tensor(rowf[:], sel[:, 0, :], float(NKEY), sel[:, 1, :], ALU.mult, ALU.add))
                                V.tensor_scalar(rowi[:, t, :], rowf[:], row_base[:, 0:1], None, ALU.add).then_inc(s_idx, 1)

                            def expert_gates(t):
                                dve.wait_ge(s_gexp, t + 1)
                                dch.link(V.tensor_reduce(gs[:, 0, :], gw[:, t], AX, ALU.add))
                                dch.link(V.reciprocal(gs[:, 1, :], gs[:, 0, :]))
                                dch.link(V.tensor_tensor(gw[:, t], gw[:, t], over(gs[:, 1, :], TOPK), ALU.mult))

                            def weight(m):
                                t, h = divmod(m, PH)
                                dve.wait_ge(s_gelu, m + 1)
                                d = dots[:, t, h * TOPK:(h + 1) * TOPK]
                                V.tensor_tensor(d, d, gw[:, t, h, :], ALU.mult).then_inc(s_w, 1)

                            for hx in range(16):
                                key_top(0, hx)
                            candidates(0)
                            for h in range(PH):
                                pair_top(h)
                            experts(0)
                            expert_gates(0)
                            for n in range(ALL):
                                t, j = divmod(n, STEPS)
                                dve.wait_ge(s_u[n % NU], 16 * (n // NU + 1))
                                V.tensor_tensor_reduce(out=ub[:, n % NU, :], in0=ub[:, n % NU, :], in1=h_tok[:, t, :], scale=1.0,
                                                       scalar=0.0, op0=ALU.mult, op1=ALU.add,
                                                       accum_out=dots[:, t, j:j + 1]).then_inc(s_dot, 1)
                                if 0 <= n < 64 and n % 4 == 3:
                                    key_top(1, n // 4)
                                if n == 64:
                                    candidates(1)
                                if 65 <= n < 65 + 4 * PH and (n - 65) % 4 == 0:
                                    pair_top((n - 65) // 4)
                                if n == 98:
                                    experts(1)
                                if n == 104:
                                    expert_gates(1)
                                if n >= TOPK and n % TOPK == 3:
                                    weight(n // TOPK - 1)
                            weight(HEADS - 1)
                            for t in range(NT):
                                dve.wait_ge(s_vacc, STEPS * (t + 1))
                                for h in range(2):
                                    xv = x[:, t, h * 512:(h + 1) * 512]
                                    V.tensor_tensor(xv, xv, bank[2 * t + h][:], ALU.add).then_inc(s_xffn, 1)
                            V.tensor_scalar(row_base[:], row_base[:], float(EXPERTS), None, ALU.add).then_inc(s_xffn, 1)
                            dve.wait_ge(s_xffn, 5)

                        @block.scalar
                        def _(act):
                            def gate_exp(t):
                                act.wait_ge(s_cand, NT + t + 1)
                                A.activation(gw[:, t], gw[:, t], ACT.Exp).then_inc(s_gexp, 1)

                            gate_exp(0)
                            for m in range(HEADS):
                                t, h = divmod(m, PH)
                                act.wait_ge(s_dot, TOPK * (m + 1))
                                d = dots[:, t, h * TOPK:(h + 1) * TOPK]
                                A.activation(d, d, ACT.Gelu_apprx_tanh).then_inc(s_gelu, 1)
                                if m == 5:
                                    gate_exp(1)
                                act.wait_ge(s_w, m + 1)
                                for k in range(TOPK):
                                    n = m * TOPK + k
                                    if n >= 4:
                                        act.wait_ge(s_vacc, n - 3)
                                    A.activation(diag[:, n % 4, :], ident, ACT.Copy,
                                                 scale=dots[:, t, h * TOPK + k:h * TOPK + k + 1]).then_inc(s_diag, 1)

                        @block.tensor
                        def _(pe):
                            for n in range(ALL):
                                t, j = divmod(n, STEPS)
                                pe.wait_ge(s_diag, n + 1)
                                pe.wait_ge(s_v[n % NU], 16 * (n // NU + 1))
                                for h in range(2):
                                    mm = PE.matmul(bank[2 * t + h][:], diag[:, n % 4, :], vb[:, n % NU, h * 512:(h + 1) * 512],
                                                   start=(j == 0), stop=(j == STEPS - 1))
                                mm.then_inc(s_vacc, 1)

            clear()

        with nc.Block(no_gpsimd_drain=True) as block:
            @block.sync
            def _(sp):
                sp.dma_start(out.rearrange("(t p) d -> p t d", p=P), x[:]).then_inc(s_store, 16)
                sp.wait_ge(s_store, 16)


def _tiles(w):
    k, n = w.shape
    return w.reshape(k // P, P, n).transpose(1, 0, 2).reshape(P, -1)


def _vectors(v):
    return v.reshape(-1, P).T


def _layout(a):
    heads = [g * NP + i for i in range(NP) for g in range(G)]
    q_cols = np.concatenate([np.arange(h * DH, (h + 1) * DH) for h in heads])
    gate_cols = np.concatenate([np.arange(3 * h, 3 * h + 3) for h in heads])
    kv = 1024 + np.arange(768).reshape(6, 128)
    ag = 1792 + gate_cols
    lx, lg, z = 1840, 2864, 3888
    xbc, dt, mg = 4912, 6448, 6464
    stream = np.zeros((L, GROUPS, P, WCOL), np.float32)
    small = np.zeros((L, P, SMALL), np.float32)
    rows = np.zeros((L, ROWS), np.float32)
    for l in range(L):
        w = a["w_in"][l]
        stream[l, KV0] = _tiles(w[:, np.concatenate([kv[0], kv[2], kv[4], kv[1]])])
        kv1 = np.concatenate([kv[3], kv[5], ag, dt + np.arange(SH)])
        stream[l, KV1, :, 0:KT * KV1_COLS] = _tiles(w[:, kv1])
        for g in range(2):
            stream[l, Q0 + g] = _tiles(w[:, q_cols[512 * g:512 * (g + 1)]])
            stream[l, LX0 + g] = _tiles(w[:, lx + 512 * g:lx + 512 * (g + 1)])
            stream[l, LG0 + g] = _tiles(w[:, lg + 512 * g:lg + 512 * (g + 1)])
            stream[l, Z0 + g] = _tiles(w[:, z + 512 * g:z + 512 * (g + 1)])
            stream[l, OUT0 + g] = _tiles(a["w_out"][l][:, 512 * g:512 * (g + 1)])
        for g in range(3):
            stream[l, XBC0 + g] = _tiles(w[:, xbc + 512 * g:xbc + 512 * (g + 1)])
        for g in range(6):
            stream[l, MG0 + g] = _tiles(w[:, mg + 512 * g:mg + 512 * (g + 1)])
            wb = a["w_branch"][l, g // 2]
            if g < 2:
                wb = wb[q_cols]
            stream[l, BR0 + g] = _tiles(wb[:, 512 * (g % 2):512 * (g % 2 + 1)])
        for g in range(4):
            stream[l, PQ0 + g] = _tiles(a["peer_w_q"][l][:, 512 * g:512 * (g + 1)])
        stream[l, W1K] = _tiles(a["cmp_k_w1"][l])
        stream[l, W1V] = _tiles(a["cmp_v_w1"][l])

        parts = {
            "mix_g": _vectors(a["mix_norm_g"][l]), "conv_w": _vectors(a["lru_conv_w"][l]),
            "conv_b": _vectors(a["lru_conv_b"][l]), "b_r": _vectors(a["lru_b_r"][l]),
            "b_i": _vectors(a["lru_b_i"][l]), "lam": _vectors(a["lru_lambda"][l]),
            "xconv_w": _vectors(a["ssm_conv_w"][l]), "xconv_b": _vectors(a["ssm_conv_b"][l]),
            "ssm_g": _vectors(a["ssm_norm_g"][l]),
            "pe": np.concatenate([_vectors(a["cmp_pe_k"][l]), _vectors(a["cmp_pe_v"][l])], 1),
        }
        for name, v in parts.items():
            small[l, :, _vec[name][0]:_vec[name][1]] = v
        wl = np.zeros((P, 2, KT, P), np.float32)
        for j, name in enumerate(("lru_w_r", "lru_w_i")):
            for h in range(16):
                o = (h % 2) * 64
                wl[o:o + 64, j, h // 2, o:o + 64] = a[name][l, h]
        small[l, :, VEC:VEC + LRU_W] = wl.reshape(P, -1)
        small[l, :, VEC + LRU_W:] = np.concatenate([_tiles(a["cmp_k_w2"][l]), _tiles(a["cmp_v_w2"][l])], 1)
        rows[l] = np.concatenate([a["ssm_dt_bias"][l], a["ssm_a_log"][l], a["ssm_d"][l], a["q_norm_g"][l], a["k_norm_g"][l]])
    sk = a["peer_sub_keys"].transpose(0, 4, 1, 2, 3).reshape(L, P, 16, P)
    return {
        "x": a["x"].reshape(S, D), "pos_tok": a["positions"].reshape(NT, P).T, "pos_row": a["positions"].reshape(S),
        "const": constants(), "wstream": stream.reshape(L * GROUPS, P, WCOL), "small": small, "rows": rows,
        "ffn_row": a["ffn_norm_g"], "subkeys": sk, "table_u": a["peer_u"].reshape(L * EXPERTS, D),
        "table_v": a["peer_v"].reshape(L * EXPERTS, D),
    }


def kernel(**inputs):
    import concourse.bacc as bacc
    from concourse.bass_utils import run_bass_kernel_spmd

    nc = bacc.Bacc("TRN2", target_bir_lowering=False, num_devices=1)
    arrays, args = {}, []
    for name, a in _layout({k: np.asarray(v) for k, v in inputs.items()}).items():
        a = np.ascontiguousarray(a)
        arrays[f"in_{name}"] = a
        args.append(nc.dram_tensor(f"in_{name}", a.shape, mybir.dt.from_np(a.dtype), kind="ExternalInput").ap())
    o = nc.dram_tensor("out_0", (S, D), F32, kind="ExternalOutput").ap()
    trunk(nc, *args, o)
    r = run_bass_kernel_spmd(nc, [arrays], core_ids=[0])
    return r.results[0]["out_0"].reshape(1, S, D)
```

```python
from contextlib import ExitStack

import numpy as np
import concourse.bass as bass
from concourse import mybir

ALU = mybir.AluOpType
ACT = mybir.ActivationFunctionType
F32 = mybir.dt.float32
I32 = mybir.dt.int32
U32 = mybir.dt.uint32
F32R = mybir.dt.float32r
AX = mybir.AxisListType.X

P = 128
D = 1024
S = 256
L = 2
NT = S // P
KT = D // P
DH = 64
G = 2
NP = 8
NCMP = 15
CROWS = 31
EPS = 1e-6
SCALE = DH ** -0.5
NEG = -1e30
HALF = DH // 2
FX = 12
CONV = 4
PAD = CONV - 1
SH = 16
PH = 8
TOPK = 16
NKEY = 128

KV0, KV1, Q0, LX0, LG0, XBC0, Z0 = 0, 1, 2, 4, 6, 8, 11
W1K, W1V, MG0 = 13, 14, 15
BR0, OUT0, PQ0 = 21, 27, 29
GROUPS = 33
PIECES = 2 * GROUPS
WCOL = 2048
RING = 4
HIS = 3
UNSPLIT = range(2 * W1K, 2 * MG0)
SHARED = range(2 * BR0, 2 * BR0 + 11)

KV_COLS = 832
VC, VS, VW, GATE, DTC = 384, 512, 640, 768, 816

_vec = {}
_at = 0
for _name, _n in (("mix_g", 8), ("conv_w", 32), ("conv_b", 8), ("b_r", 8), ("b_i", 8), ("lam", 8),
                  ("xconv_w", 48), ("xconv_b", 12), ("ssm_g", 8), ("pe", 32)):
    _vec[_name] = (_at, _at + _n)
    _at += _n
VEC = _at
LRU_W = 2 * KT * P
W2 = 2 * 2 * DH
SMALL = VEC + LRU_W + W2
ROW_DTB, ROW_ALOG, ROW_D, ROW_QG, ROW_KG, ROWS = 0, 16, 32, 48, 112, 176
C_ID, C_UP, C_STRICT, C_CAUSAL, C_CMPB, C_CMPM, C_INV, C_IOTA, CONSTS = (
    0, 128, 256, 384, 640, 672, 704, 736, 864)
TWO_PI = 2 * np.pi
PI_A = 6.28125
PI_B = float(np.float32(np.float32(round((TWO_PI - PI_A) * 2 ** 21)) / 2 ** 21))
PI_C = float(TWO_PI - PI_A - PI_B)
ROUND = 1.5 * 2 ** 23
SIN_MAX = 3.1415925
STEPS = PH * TOPK
XR = 4
EARLY = 44
GB = 4
EXPERT_SMALL = 4 * (2 * XR * D + 2 * 512 + 2 * 2 * GB * P + 3 * S)


def constants():
    c = np.zeros((P, CONSTS), np.float32)
    k, j = np.arange(P)[:, None], np.arange(P)[None, :]
    c[:, C_ID:C_ID + P] = k == j
    c[:, C_UP:C_UP + P] = k <= j
    c[:, C_STRICT:C_STRICT + P] = k > j
    c[:, C_CAUSAL + P:C_CAUSAL + 2 * P] = np.where(j > k, NEG, 0)
    for t in range(NT):
        end = 16 * np.arange(NCMP)[None, :] + 31
        ok = end <= k + t * P
        c[:, C_CMPB + 16 * t:C_CMPB + 16 * t + NCMP] = np.where(ok, 0, NEG)
        c[:, C_CMPM + 16 * t:C_CMPM + 16 * t + NCMP] = ok
    c[:, C_INV:C_INV + HALF] = np.float32(10000.0) ** (-np.arange(HALF, dtype=np.float32) / HALF)
    c[:, C_IOTA:C_IOTA + NKEY] = np.arange(NKEY)
    return c


class Chain:

    def __init__(self, eng, sem):
        self.eng, self.sem, self.n = eng, sem, 0

    def add(self, ins):
        ins.then_inc(self.sem, 1)
        self.n += 1

    def settle(self):
        self.eng.wait_ge(self.sem, self.n)

    def link(self, ins):
        self.add(ins)
        self.settle()


def over(ap, n):
    return ap.unsqueeze(2).to_broadcast([ap.shape[0], ap.shape[1], n])


def times(ap, n):
    return ap.unsqueeze(1).to_broadcast([ap.shape[0], n, ap.shape[1]])


def trunk(nc, x_in, pos_tok, pos_row, const, wstream, small, rows, ffn_row, subkeys, xstream, out):
    V, A, PE, PO = nc.vector, nc.scalar, nc.tensor, nc.gpsimd
    with ExitStack() as ctx:
        def sb(name, shape, dt=F32, where=ctx):
            return where.enter_context(nc.sbuf_tensor(name, shape, dt))

        sems = {}

        def sem(name):
            sems[name] = ctx.enter_context(nc.semaphore(name))
            return sems[name]

        bank = [ctx.enter_context(nc.psum_tensor(f"bank{i}", [P, 512], F32)) for i in range(8)]

        cst = sb("cst", [P, CONSTS])
        ident = cst[:, C_ID:C_ID + P]
        upper = cst[:, C_UP:C_UP + P]
        strict = cst[:, C_STRICT:C_STRICT + P]
        x = sb("x", [P, NT, D])
        featH, featL = sb("featH", [P, KT, S], F32R), sb("featL", [P, KT, S], F32R)
        rope_c = sb("rope_c", [P, NT, DH])
        rope_s = sb("rope_s", [P, NT, DH])
        not_reset = sb("not_reset", [P, S])
        is_reset = sb("is_reset", [P, S])
        eps = sb("eps", [P, 1])
        st = sb("st", [P, 64])
        layer_at = nc.sbuf_base

        s_in = sem("inputs_loaded")
        s_setup = sem("setup")
        loaded = [sem(f"weights_loaded_{i}") for i in range(RING)]
        s_small = sem("small_loaded")
        s_rows = sem("rows_loaded")
        s_subk = sem("subkeys_loaded")
        s_dve, s_act, s_pool = sem("dve_chain"), sem("act_chain"), sem("pool_chain")
        s_hi, s_lo_pool, s_lo_dve = sem("weight_hi"), sem("weight_lo_pool"), sem("weight_lo_dve")
        s_proj, s_evac = sem("unit_multiplied"), sem("unit_taken")
        s_y0, s_y1 = sem("branch_hi"), sem("branch_split")
        s_ssq, s_nrm, s_nt, s_ntev = sem("norm_root"), sem("x_normed"), sem("x_turned"), sem("xT_taken")
        s_kr, s_krt = sem("k_squares"), sem("k_root")
        s_qr, s_qrt = sem("q_squares"), sem("q_root")
        s_sp, s_spe = sem("softplus_in"), sem("softplus_exp")
        s_pads = sem("pads_zero")
        s_conv, s_lg, s_lgev = sem("lru_conv"), sem("lru_gate_multiplied"), sem("lru_gate_taken")
        s_la, s_lexp, s_lm, s_lsq = sem("lru_log_a"), sem("lru_exp"), sem("lru_one_minus_a2"), sem("lru_root")
        s_xconv, s_silu = sem("ssm_conv"), sem("ssm_silu")
        s_kvt, s_kvtev, s_qt, s_qtev = sem("kv_turned"), sem("kvT_taken"), sem("q_turned"), sem("qT_taken")
        s_ch, s_chg, s_cht, s_chtev = (sem("cmp_hidden"), sem("cmp_gelu"), sem("cmp_hidden_turned"),
                                       sem("cmp_hiddenT_taken"))
        s_co, s_cksq, s_ckrt, s_ckn = sem("cmp_out"), sem("cmp_k_squares"), sem("cmp_k_root"), sem("cmp_k_normed")
        s_ckt, s_cktev = sem("cmp_k_turned"), sem("cmp_kT_taken")
        s_cs, s_cmask, s_cexp, s_cp = (sem("cmp_scores"), sem("cmp_masked"), sem("cmp_exp"), sem("cmp_probs"))
        s_sig = sem("gates_sigmoid")
        s_sc, s_sctk, s_max, s_exp = sem("scores"), sem("scores_taken"), sem("row_max"), sem("row_exp")
        s_coef, s_scaled = sem("coefficients"), sem("probs_scaled")
        s_pt, s_ptev_a, s_ptev_v = sem("probs_turned"), sem("probsT_taken_act"), sem("probsT_taken_dve")
        s_y, s_yev = sem("attended"), sem("attended_taken")
        s_ea, s_adt, s_sd, s_sde = sem("exp_a"), sem("adt"), sem("ssd_sums"), sem("ssd_sums_exp")
        s_xt, s_xtev, s_xd = sem("xs_turned"), sem("xs_taken"), sem("x_times_dt")
        s_cb, s_cbm, s_au = sem("cb"), sem("cb_masked"), sem("adt_upper")
        s_seg, s_dec, s_m = sem("segsum"), sem("decay"), sem("cb_times_decay")
        s_yd, s_ydtk = sem("ssd_y"), sem("ssd_y_taken")
        s_s0, s_s0ev, s_yo, s_yotk = sem("state"), sem("state_taken"), sem("y_off"), sem("y_off_taken")
        s_zy, s_zrt, s_zn, s_zt, s_ztev = (sem("gated_y"), sem("gated_root"), sem("gated_normed"),
                                           sem("gated_turned"), sem("gatedT_taken"))
        s_mgs, s_mrg, s_xout = sem("merge_sigmoid"), sem("merged"), sem("x_mixed")
        s_hrow = sem("ffn_row_loaded")
        s_hrt, s_hn, s_ht, s_htev = sem("h_root"), sem("h_normed"), sem("h_turned"), sem("hT_taken")
        s_ps, s_psev = sem("key_scores"), sem("key_scores_taken")
        s_cand, s_gexp = sem("candidates"), sem("expert_softmax_exp")
        s_chosen, s_gt, s_gttk = sem("experts_chosen"), sem("choice_turned"), sem("choiceT_taken")
        s_xl = [sem(f"expert_weights_loaded_{i}") for i in range(XR)]
        s_xhi, s_xlo_pool, s_xlo_dve = sem("expert_weight_hi"), sem("expert_weight_lo_pool"), sem("expert_weight_lo_dve")
        s_xu, s_uev, s_gated = sem("expert_unit_multiplied"), sem("expert_gelu"), sem("expert_gated")
        s_hot, s_wp, s_wa = sem("one_hots"), sem("one_hots_weighted_pool"), sem("one_hots_weighted_act")
        s_gates = sem("gates_spread")
        s_gev_v, s_gev_a = sem("gates_taken_dve"), sem("gates_taken_act")
        s_phi, s_plo, s_xffn = sem("probs_hi"), sem("probs_lo"), sem("x_ffn")
        s_store = sem("stored")

        with ExitStack() as tmp:
            pt = sb("pt", [P, NT], I32, tmp)
            ptf = sb("ptf", [P, NT], F32, tmp)
            pr = sb("pr", [P, S], I32, tmp)
            prf = sb("prf", [P, S], F32, tmp)
            ang = sb("ang", [P, NT, HALF], F32, tmp)
            turn = sb("turn", [P, 2, NT, HALF], F32, tmp)
            arg = sb("arg", [P, 2, NT, HALF], F32, tmp)
            trig = sb("trig", [P, 2, NT, HALF], F32, tmp)
            with nc.Block(no_gpsimd_drain=True) as block:
                @block.sync
                def _(sp):
                    sp.dma_start(cst[:], const).then_inc(s_in, 16)
                    sp.dma_start(pt[:], pos_tok).then_inc(s_in, 16)
                    sp.dma_start(pr[:], pos_row.partition_broadcast(P)).then_inc(s_in, 16)
                    sp.dma_start(x[:], x_in.rearrange("(t p) d -> p t d", p=P)).then_inc(s_in, 16)

                @block.vector
                def _(dve):
                    ch = Chain(dve, s_dve)
                    V.memset(eps[:], EPS)
                    dve.wait_ge(s_in, 64)
                    V.tensor_copy(ptf[:], pt[:])
                    ch.link(V.tensor_copy(prf[:], pr[:]))
                    V.tensor_scalar(not_reset[:], prf[:], 0.0, None, ALU.not_equal)
                    V.tensor_scalar(is_reset[:], prf[:], 0.0, None, ALU.is_equal)
                    ch.link(V.tensor_tensor(ang[:], over(ptf[:], HALF),
                                            times(cst[:, C_INV:C_INV + HALF], NT), ALU.mult))
                    for j in range(2):
                        V.tensor_scalar(arg[:, j], ang[:], 1 / TWO_PI, 0.25 * j, ALU.mult, ALU.add).then_inc(s_dve, 1)
                        ch.n += 1
                    ch.settle()
                    ch.link(V.tensor_scalar(turn[:], arg[:], ROUND, None, ALU.add))
                    ch.link(V.tensor_scalar(turn[:], turn[:], -ROUND, None, ALU.add))
                    for j in range(2):
                        ch.add(V.scalar_tensor_tensor(arg[:, j], turn[:, j], -PI_A, ang[:], ALU.mult, ALU.add))
                    ch.settle()
                    ch.link(V.scalar_tensor_tensor(arg[:], turn[:], -PI_B, arg[:], ALU.mult, ALU.add))
                    ch.link(V.scalar_tensor_tensor(arg[:], turn[:], -PI_C, arg[:], ALU.mult, ALU.add))
                    ch.link(V.tensor_scalar(arg[:, 1], arg[:, 1], np.pi / 2, None, ALU.add))
                    V.tensor_scalar(arg[:], arg[:], SIN_MAX, -SIN_MAX, ALU.min, ALU.max).then_inc(s_setup, 1)
                    dve.wait_ge(s_setup, 2)
                    V.tensor_copy(rope_c[:, :, 0:HALF], trig[:, 1])
                    V.tensor_copy(rope_c[:, :, HALF:DH], trig[:, 1])
                    V.tensor_scalar(rope_s[:, :, 0:HALF], trig[:, 0], -1.0, None, ALU.mult)
                    V.tensor_copy(rope_s[:, :, HALF:DH], trig[:, 0]).then_inc(s_setup, 1)
                    dve.wait_ge(s_setup, 3)

                @block.scalar
                def _(act):
                    act.wait_ge(s_setup, 1)
                    A.activation(trig[:], arg[:], ACT.Sin).then_inc(s_setup, 1)

        all_sems = list(sems.values())
        first, last_sem = min(q.num for q in all_sems), max(q.num for q in all_sems)

        def clear():
            nc.gpsimd.dma_reset(range(first, last_sem + 1))
            nc.all_engine_barrier(sem_only=True)
            nc.sync.sem_clear(range(first, last_sem + 1))
            nc.all_engine_barrier(sem_only=True)

        clear()

        with nc.Fori(0, L) as layer:
            wide = ExitStack()
            ring = sb("ring", [P, RING, WCOL], F32, wide)
            ring_lo = nc.alloc_sbuf_tensor_at("ring_lo", [P, RING, WCOL], F32R, offset=layer_at)
            ring_hi = sb("ring_hi", [P, HIS, WCOL], F32R, wide)
            dch, ach, pch = Chain(V, s_dve), Chain(A, s_act), Chain(PO, s_pool)

            def nth(u):
                return u if u < UNSPLIT.start else u - len(UNSPLIT)

            def piece(n):
                return n if n < UNSPLIT.start else n + len(UNSPLIT)

            def load(sp, u):
                if u >= RING:
                    sp.wait_ge(s_proj, u - RING + 1)
                sp.dma_start(ring[:, u % RING], wstream[bass.ds(layer * PIECES + u, 1)].rearrange("a p c -> (a p) c")
                             ).then_inc(loaded[u % RING], 16)

            def arrived(eng, u):
                eng.wait_ge(loaded[u % RING], 16 * (u // RING + 1))

            def split_hi(act, u):
                if u >= PIECES:
                    return
                arrived(act, u)
                if nth(u) >= HIS:
                    act.wait_ge(s_proj, piece(nth(u) - HIS) + 1)
                A.activation(ring_hi[:, nth(u) % HIS], ring[:, u % RING], ACT.Copy).then_inc(s_hi, 1)

            def on_pool(u):
                return u < SHARED.start or u in SHARED and u % 2 == 0

            def lo_count(u):
                return sum(on_pool(v) == on_pool(u) for v in range(u + 1) if v not in UNSPLIT)

            def split_lo(eng, u):
                if u >= PIECES:
                    return
                eng.wait_ge(s_hi, nth(u) + 1)
                (PO if on_pool(u) else V).tensor_tensor(
                    ring_lo[:, u % RING], ring[:, u % RING], ring_hi[:, nth(u) % HIS].bitcast(F32), ALU.subtract
                ).then_inc(s_lo_pool if on_pool(u) else s_lo_dve, 1)

            def is_split(pe, u):
                pe.wait_ge(s_lo_pool if on_pool(u) else s_lo_dve, lo_count(u))
                cut3 = "p (k c) -> p k c"
                return (ring_hi[:, nth(u) % HIS].rearrange(cut3, k=KT), ring_lo[:, u % RING].rearrange(cut3, k=KT))

            def three_passes(o, s_hi_lo, m_hi_lo, first, last):
                PE.matmul(o, s_hi_lo[0], m_hi_lo[0], start=first, stop=False)
                PE.matmul(o, s_hi_lo[0], m_hi_lo[1], start=False, stop=False)
                return PE.matmul(o, s_hi_lo[1], m_hi_lo[0], start=False, stop=last)

            def token_unit(pe, u, src, nb, cols=256):
                w = is_split(pe, u)
                for t in range(NT):
                    for k in range(KT):
                        mm = three_passes(bank[u % nb][:, t * cols:(t + 1) * cols],
                                          [a[:, k, t * P:(t + 1) * P] for a in src], [a[:, k, 0:cols] for a in w],
                                          k == 0, k == KT - 1)
                mm.then_inc(s_proj, 1)

            def feature_half(pe, u, f, src, o):
                w = is_split(pe, u)
                for k in range(KT):
                    mm = three_passes(o, [a[:, k, f * P:(f + 1) * P] for a in w], [a[:, k, :] for a in src],
                                      k == 0, k == KT - 1)
                return mm

            def feature_unit(pe, u, src, nb):
                for f in range(2):
                    mm = feature_half(pe, u, f, src, bank[u % nb][:, f * S:(f + 1) * S])
                mm.then_inc(s_proj, 1)

            feat = (featH, featL)

            mix = ExitStack()
            with mix:
                tok_q_at = nc.sbuf_base
                tok_q = sb("tok_q", [P, NT, D], F32, mix)
                lgT_at = nc.sbuf_base
                lgT = sb("lgT", [P, KT, S], F32, mix)
                lgH = nc.alloc_sbuf_tensor_at("lgH", [P, KT, S], F32R, offset=tok_q_at)
                lgL = nc.alloc_sbuf_tensor_at("lgL", [P, KT, S], F32R, offset=lgT_at)
                big = sb("big", [P, 3 * KT * S], F32, mix)
                smw = sb("smw", [P, SMALL], F32, mix)
                row = sb("row", [P, ROWS], F32, mix)
                sp_x = sb("sp_x", [P, 6, 40], F32, mix)
                expa = sb("expa", [P, SH], F32, mix)
                adt = sb("adt", [P, NT, SH], F32, mix)
                qT = sb("qT", [P, NP, S], F32, mix)
                early = mix.enter_context(ExitStack())
                tok_kv = sb("tok_kv", [P, NT, KV_COLS], F32, early)
                tok_z = sb("tok_z", [P, NT, D], F32, early)
                lxT = sb("lxT", [P, KT, S + PAD], F32, early)
                xbcT = sb("xbcT", [P, FX, S + PAD], F32, early)
                xbcC = sb("xbcC", [P, FX, S], F32, early)
                xcT = sb("xcT", [P, KT, S], F32, early)

                mgT = big[:].rearrange("p (f s) -> p f s", f=3 * KT)
                normed = big[:, 0:NT * D].rearrange("p (t d) -> p t d", t=NT)
                scr_a, scr_b = big[:, 2048:3072], big[:, 3072:4096]
                scr_act = big[:, 4096:5120]
                raw_xT = big[:, 4096:6144].rearrange("p (f s) -> p f s", f=KT)
                gate_r = big[:, 0:2048].rearrange("p (f s) -> p f s", f=KT)
                gate_i = big[:, 2048:4096].rearrange("p (f s) -> p f s", f=KT)
                lru_a = big[:, 4096:6144].rearrange("p (f s) -> p f s", f=KT)
                a_sq = lxT[:].rearrange("p f s -> p (f s)")[:, 0:KT * S].rearrange("p (f s) -> p f s", f=KT)
                sp_arg, sp_e, sp_w, sp_w2, sp_p, sp_out = (sp_x[:, j] for j in range(6))
                dt = sp_out[:, 0:2 * SH].rearrange("p (t h) -> p t h", t=NT)
                lru_c = sp_out[:, 32:40]

                def vec(name):
                    return smw[:, _vec[name][0]:_vec[name][1]]

                w_lru = smw[:, VEC:VEC + LRU_W].rearrange("p (j f c) -> p j f c", j=2, f=KT)
                w2 = smw[:, VEC + LRU_W:SMALL].rearrange("p (j k c) -> p j k c", j=2, k=2)

                NB = 4
                with nc.Block(no_gpsimd_drain=True) as block:
                    @block.sync
                    def _(sp):
                        load(sp, 0)
                        sp.dma_start(smw[:], small[bass.ds(layer, 1)].rearrange("a p c -> (a p) c")).then_inc(s_small, 16)
                        sp.dma_start(row[:], rows[bass.ds(layer, 1)].rearrange("a c -> (a c)").partition_broadcast(P)
                                     ).then_inc(s_rows, 16)
                        for u in range(1, UNSPLIT.stop):
                            load(sp, u)

                    @block.tensor
                    def _(pe):
                        for t in range(NT):
                            pe.wait_ge(s_nrm, t + 1)
                            for h in range(2):
                                if t:
                                    pe.wait_ge(s_ntev, h + 1)
                                for j in range(4):
                                    tr = PE.transpose(bank[6 + h][:, j * P:(j + 1) * P],
                                                      normed[:, t, (4 * h + j) * P:(4 * h + j + 1) * P], ident)
                                tr.then_inc(s_nt, 1)
                        pe.wait_ge(s_ntev, 4)

                        def free(u):
                            if u >= NB:
                                pe.wait_ge(s_evac, u - NB + 1)

                        for u in range(2 * LX0):
                            free(u)
                            token_unit(pe, u, feat, NB, 64 if u == 2 * KV1 + 1 else 256)
                        for u in range(2 * LX0, 2 * XBC0 + 2):
                            free(u)
                            feature_unit(pe, u, feat, NB)
                        pe.wait_ge(s_conv, 1)
                        for f in range(KT):
                            if f >= 2:
                                pe.wait_ge(s_lgev, f - 1)
                            for j in range(2):
                                mm = PE.matmul(bank[4 + f % 2][:, j * S:(j + 1) * S], w_lru[:, j, f, :], xcT[:, f, :],
                                               start=True, stop=True)
                            mm.then_inc(s_lg, 1)
                        for u in range(2 * XBC0 + 2, 2 * Z0):
                            free(u)
                            feature_unit(pe, u, feat, NB)
                        for u in range(2 * Z0, 2 * W1K):
                            free(u)
                            token_unit(pe, u, feat, NB)

                    @block.scalar
                    def _(act):
                        for t in range(NT):
                            ach.link(A.activation(scr_act[:], x[:, t, :], ACT.Square, accum_out=st[:, t:t + 1]))
                        A.activation(st[:, 2:4], st[:, 0:2], ACT.Sqrt, bias=eps[:], scale=1 / D).then_inc(s_ssq, 1)
                        for u in range(HIS):
                            split_hi(act, u)

                        def take(u, dst, func=ACT.Copy, cols=256):
                            act.wait_ge(s_proj, u + 1)
                            A.activation(dst, bank[u % NB][:, 0:2 * cols].rearrange("p (f s) -> p f s", f=2),
                                         func).then_inc(s_evac, 1)
                            if u + HIS < UNSPLIT.start:
                                split_hi(act, u + HIS)

                        for n in range(3):
                            take(2 * KV0 + n, tok_kv[:, :, 256 * n:256 * (n + 1)])
                        take(2 * KV1 + 1, tok_kv[:, :, 768:KV_COLS], cols=64)
                        for n in range(4):
                            take(2 * Q0 + n, tok_q[:, :, 256 * n:256 * (n + 1)])
                            if n == 0:
                                for t in range(NT):
                                    act.wait_ge(s_kr, t + 1)
                                    A.activation(st[:, 8 + 6 * t:14 + 6 * t], st[:, 8 + 6 * t:14 + 6 * t], ACT.Sqrt,
                                                 scale=1 / DH).then_inc(s_krt, 1)
                        act.wait_ge(s_sp, 1)
                        A.activation(sp_e, sp_e, ACT.Exp).then_inc(s_spe, 1)
                        act.wait_ge(s_rows, 16)
                        A.activation(expa[:], row[:, ROW_ALOG:ROW_ALOG + SH], ACT.Exp).then_inc(s_ea, 1)
                        act.wait_ge(s_pads, 2)
                        for n in range(4):
                            take(2 * LX0 + n, lxT[:, 2 * n:2 * n + 2, PAD:])
                            if n == 0:
                                for t in range(NT):
                                    act.wait_ge(s_qr, t + 1)
                                    A.activation(st[:, 20 + 16 * t:36 + 16 * t], st[:, 20 + 16 * t:36 + 16 * t], ACT.Sqrt,
                                                 scale=1 / DH).then_inc(s_qrt, 1)
                        for n in range(4):
                            take(2 * LG0 + n, lgT[:, 2 * n:2 * n + 2, :], ACT.Gelu_apprx_tanh)
                        for n in range(2):
                            take(2 * XBC0 + n, xbcT[:, 2 * n:2 * n + 2, PAD:])
                        for f in range(KT):
                            act.wait_ge(s_lg, f + 1)
                            A.activation(gate_r[:, f, :], bank[4 + f % 2][:, 0:S], ACT.Sigmoid,
                                         bias=vec("b_r")[:, f:f + 1])
                            A.activation(gate_i[:, f, :], bank[4 + f % 2][:, S:2 * S], ACT.Sigmoid,
                                         bias=vec("b_i")[:, f:f + 1]).then_inc(s_lgev, 1)
                        for n in range(2, 6):
                            take(2 * XBC0 + n, xbcT[:, 2 * n:2 * n + 2, PAD:])
                            if n == 2:
                                act.wait_ge(s_la, 1)
                                A.activation(lru_a[:], gate_r[:], ACT.Exp, scale=-1.0).then_inc(s_lexp, 1)
                                A.activation(gate_r[:], gate_r[:], ACT.Tanh).then_inc(s_lexp, 1)
                            if n == 4:
                                act.wait_ge(s_lm, 1)
                                A.activation(gate_r[:], gate_r[:], ACT.Sqrt).then_inc(s_lsq, 1)
                        for n in range(4):
                            take(2 * Z0 + n, tok_z[:, :, 256 * n:256 * (n + 1)], ACT.Silu)
                        act.wait_ge(s_xconv, 1)
                        for n in range(3):
                            A.activation(xbcC[:, 4 * n:4 * n + 4, :], xbcC[:, 4 * n:4 * n + 4, :], ACT.Silu).then_inc(s_silu, 1)
                        act.wait_ge(s_silu, 3)

                    @block.gpsimd
                    def _(pool):
                        for u in range(UNSPLIT.start):
                            split_lo(pool, u)

                    @block.vector
                    def _(dve):
                        V.memset(lxT[:, :, 0:PAD], 0.0).then_inc(s_pads, 1)
                        V.memset(xbcT[:, :, 0:PAD], 0.0).then_inc(s_pads, 1)
                        dve.wait_ge(s_ssq, 1)
                        dch.link(V.reciprocal(st[:, 4:6], st[:, 2:4]))
                        for t in range(NT):
                            V.tensor_scalar(normed[:, t, :], x[:, t, :], st[:, 4 + t:5 + t], None, ALU.mult).then_inc(s_nrm, 1)
                        dve.wait_ge(s_small, 16)
                        dve.wait_ge(s_rows, 16)
                        for t in range(NT):
                            for h in range(2):
                                dve.wait_ge(s_nt, 2 * t + h + 1)
                                at = (slice(None), slice(4 * h, 4 * h + 4), slice(t * P, (t + 1) * P))
                                dch.link(V.tensor_tensor(raw_xT[at], bank[6 + h][:].rearrange("p (f s) -> p f s", f=4),
                                                         over(vec("mix_g")[:, 4 * h:4 * h + 4], P), ALU.mult))
                                dch.link(V.tensor_copy(featH[at], raw_xT[at]))
                                V.tensor_tensor(featL[at], raw_xT[at], featH[at].bitcast(F32), ALU.subtract).then_inc(s_ntev, 1)

                        def head_squares(src, nh, at, squares):
                            a = scr_a[:, 0:nh * DH].rearrange("p (h d) -> p h d", h=nh)
                            v = src.rearrange("p (h d) -> p h d", h=nh)
                            ss = st[:, at:at + nh]
                            dch.link(V.tensor_tensor(a, v, v, ALU.mult))
                            dch.link(V.tensor_reduce(ss, a, AX, ALU.add))
                            dch.add(V.tensor_scalar(ss, ss, DH * EPS, None, ALU.add))
                            dch.settle()
                            dve.sem_inc(squares, 1)

                        def head_norm_rope(src, nh, at, gain, root, t):
                            v = src.rearrange("p (h d) -> p h d", h=nh)
                            a = scr_a[:, 0:nh * DH].rearrange("p (h d) -> p h d", h=nh)
                            b = scr_b[:, 0:nh * DH].rearrange("p (h d) -> p h d", h=nh)
                            ss = st[:, at:at + nh]
                            dve.wait_ge(root, t + 1)
                            dch.link(V.reciprocal(ss, ss))
                            dch.link(V.tensor_tensor(v, v, over(ss, DH), ALU.mult))
                            dch.link(V.tensor_tensor(v, v, times(gain, nh), ALU.mult))
                            dch.add(V.tensor_tensor(a, v, times(rope_c[:, t, :], nh), ALU.mult))
                            dch.add(V.tensor_tensor(b[:, :, 0:HALF], v[:, :, HALF:DH],
                                                    times(rope_s[:, t, 0:HALF], nh), ALU.mult))
                            dch.link(V.tensor_tensor(b[:, :, HALF:DH], v[:, :, 0:HALF],
                                                     times(rope_s[:, t, HALF:DH], nh), ALU.mult))
                            dch.link(V.tensor_tensor(v, a, b, ALU.add))

                        dve.wait_ge(s_evac, 4)
                        for t in range(NT):
                            head_squares(tok_kv[:, t, 0:384], 6, 8 + 6 * t, s_kr)
                        for t in range(NT):
                            dch.add(V.tensor_tensor(sp_arg[:, t * SH:(t + 1) * SH], tok_kv[:, t, DTC:DTC + SH],
                                                    row[:, ROW_DTB:ROW_DTB + SH], ALU.add))
                        dch.link(V.tensor_scalar(sp_arg[:, 32:40], vec("lam"), -1.0, None, ALU.mult))
                        dch.link(V.scalar_tensor_tensor(sp_e, sp_arg, -1.0, sp_arg, ALU.mult, ALU.min))
                        V.tensor_scalar(sp_out, sp_arg, 0.0, None, ALU.max).then_inc(s_sp, 1)
                        for t in range(NT):
                            head_norm_rope(tok_kv[:, t, 0:384], 6, 8 + 6 * t, row[:, ROW_KG:ROW_KG + DH], s_krt, t)
                        dve.wait_ge(s_spe, 1)
                        dch.link(V.tensor_scalar(sp_w, sp_e, 2.0, None, ALU.add))
                        dch.link(V.reciprocal(sp_w, sp_w))
                        dch.link(V.tensor_tensor(sp_w, sp_w, sp_e, ALU.mult))
                        dch.link(V.tensor_tensor(sp_w2, sp_w, sp_w, ALU.mult))
                        dch.link(V.tensor_scalar(sp_p, sp_w2, 1 / 15, None, ALU.mult))
                        for n in (13, 11, 9, 7, 5, 3):
                            dch.link(V.scalar_tensor_tensor(sp_p, sp_p, 1 / n, sp_w2, ALU.add, ALU.mult))
                        dch.link(V.scalar_tensor_tensor(sp_p, sp_p, 1.0, sp_w, ALU.add, ALU.mult))
                        dch.link(V.scalar_tensor_tensor(sp_out, sp_p, 2.0, sp_out, ALU.mult, ALU.add))
                        dch.add(V.tensor_scalar(lru_c, lru_c, 8.0, None, ALU.mult))
                        dve.wait_ge(s_ea, 1)
                        dch.add(V.scalar_tensor_tensor(adt[:], dt, -1.0, times(expa[:], NT), ALU.mult, ALU.mult))
                        dve.wait_ge(s_evac, 8)
                        for t in range(NT):
                            head_squares(tok_q[:, t, :], 16, 20 + 16 * t, s_qr)
                        for t in range(NT):
                            head_norm_rope(tok_q[:, t, :], 16, 20 + 16 * t, row[:, ROW_QG:ROW_QG + DH], s_qrt, t)

                        def conv(dst, src, n, w, b, tiles):
                            for k in range(CONV):
                                for f in tiles:
                                    wk = w[:, k * n + f:k * n + f + 1]
                                    if k == 0:
                                        ins = V.tensor_scalar(dst[:, f, :], src[:, f, 0:S], wk, b[:, f:f + 1], ALU.mult, ALU.add)
                                    else:
                                        ins = V.scalar_tensor_tensor(dst[:, f, :], src[:, f, k:k + S], wk, dst[:, f, :],
                                                                     ALU.mult, ALU.add)
                                    dch.add(ins)
                                dch.settle()

                        dve.wait_ge(s_evac, 12)
                        conv(xcT, lxT, KT, vec("conv_w"), vec("conv_b"), range(KT))
                        dve.sem_inc(s_conv, 1)
                        dve.wait_ge(s_lgev, KT)
                        V.tensor_tensor(gate_r[:], gate_r[:], over(lru_c, S), ALU.mult).then_inc(s_la, 1)
                        dch.link(V.tensor_tensor(gate_i[:], gate_i[:], xcT[:], ALU.mult))
                        dve.wait_ge(s_evac, 18)
                        conv(xbcC, xbcT, FX, vec("xconv_w"), vec("xconv_b"), range(4))
                        dve.wait_ge(s_lexp, 2)
                        dch.link(V.tensor_tensor(a_sq, lru_a[:], lru_a[:], ALU.mult))
                        dch.link(V.scalar_tensor_tensor(gate_r[:], a_sq, 1.0, gate_r[:], ALU.add, ALU.mult))
                        V.tensor_scalar(gate_r[:], gate_r[:], 1e-30, None, ALU.max).then_inc(s_lm, 1)
                        dch.link(V.tensor_tensor(lru_a[:], lru_a[:], times(not_reset[:], KT), ALU.mult))
                        dve.wait_ge(s_lsq, 1)
                        dch.link(V.tensor_tensor(gate_r[:], gate_r[:], times(not_reset[:], KT), ALU.mult))
                        dch.link(V.tensor_tensor(gate_r[:], gate_r[:], times(is_reset[:], KT), ALU.add))
                        dch.link(V.tensor_tensor(gate_i[:], gate_i[:], gate_r[:], ALU.mult))
                        for f in range(KT):
                            dch.add(V.tensor_tensor_scan(xcT[:, f, :], lru_a[:, f, :], gate_i[:, f, :], 0.0,
                                                         ALU.mult, ALU.add))
                        dch.settle()
                        dve.wait_ge(s_evac, 16)
                        dch.link(V.tensor_tensor(lgT[:], lgT[:], xcT[:], ALU.mult))
                        dve.wait_ge(s_evac, 22)
                        conv(xbcC, xbcT, FX, vec("xconv_w"), vec("xconv_b"), range(4, FX))
                        dve.sem_inc(s_xconv, 1)

                mid = ExitStack()
                with mid:
                    kT = sb("kT", [P, 2, S], F32, mid)
                    vcmp = sb("vcmp", [NCMP, 2 * DH], F32, mid)
                    kcmpT = sb("kcmpT", [P, NCMP], F32, mid)
                    gsig = sb("gsig", [P, NT, 48], F32, mid)
                    rst = sb("rst", [P, 2, 3, 4], F32, mid)
                    cst2 = sb("cst2", [P, 3, SH], F32, mid)
                    ssd_e = sb("ssd_e", [P, NT, 2 * SH], F32, mid)
                    kst = sb("kst", [NCMP, 4], F32, mid)

                    yaT = tok_q[:].rearrange("p t d -> p (t d)").rearrange("p (f s) -> p f s", f=KT)
                    ycT = qT
                    xc_flat = xcT[:].rearrange("p f s -> p (f s)")
                    flat = xbcT[:].rearrange("p f s -> p (f s)")
                    lx_free = lxT[:].rearrange("p f s -> p (f s)")
                    sc = xc_flat.rearrange("p (b j k) -> p b j k", b=2, j=4)
                    pT = flat[:, 0:2048].rearrange("p (b k c) -> p b k c", b=2, k=2)
                    pc = lx_free[:, 0:256].rearrange("p (h c) -> p h c", h=16)
                    pcT = lx_free[0:NCMP, 256:768].rearrange("p (b c) -> p b c", b=2)
                    cT = lx_free[:, 0:1024].rearrange("p (j g s) -> p j g s", j=2, g=G)
                    blocks = lx_free[:, 0:1024].rearrange("p (j s) -> p j s", j=2)
                    chid = lx_free[0:CROWS, 1024:1536]
                    chT = lx_free[:, 1536:1536 + 4 * CROWS].rearrange("p (j c) -> p j c", j=4)
                    ck = lx_free[0:NCMP, 1664:1792]
                    cksq = lx_free[0:NCMP, 1792:1920]
                    xs_tok = xc_flat.rearrange("p (t d) -> p t d", t=NT)
                    xdt = flat[:, 0:2048].rearrange("p (t d) -> p t d", t=NT)
                    xdec = flat[:, 2048:3072]
                    q_flat = qT[:].rearrange("p f s -> p (f s)")
                    kv_flat = tok_kv[:].rearrange("p t c -> p (t c)")
                    b_tok = lx_free[:, 1024:1280].rearrange("p (g n) -> p g n", g=G)
                    cbm = lx_free[:, 1280:1792].rearrange("p (c g l) -> p c g l", c=NT, g=G)
                    au = q_flat[:, 0:1024].rearrange("p (b h l) -> p b h l", b=2, h=4)
                    dec = q_flat[:, 1024:2048].rearrange("p (b h l) -> p b h l", b=2, h=4)
                    s0 = kv_flat[:, 0:1024].rearrange("p (g c) -> p g c", g=G)
                    yt = kv_flat[:, 1024:1536]
                    yt2 = lx_free[:, 0:512]
                    zsq = lx_free[:, 512:1024]
                    units = [(t, i) for t in range(NT) for i in range(NP)]
                    MGU = 2 * MG0
                    NMG = 12
                    BU = 2 * BR0
                    EV0 = 26 + NMG

                    with nc.Block(no_gpsimd_drain=True) as block:
                        @block.sync
                        def _(sp):
                            for u in range(UNSPLIT.stop, BU + 8 + RING):
                                load(sp, u)

                        @block.tensor
                        def _(pe):
                            def gates(n):
                                if n < NMG:
                                    u = MGU + n
                                    if n >= 2:
                                        pe.wait_ge(s_evac, 26 + n - 1)
                                    feature_unit(pe, u, feat, 2)

                            for t in range(NT):
                                for j, c in enumerate((0, 128, 256, VC)):
                                    tr = PE.transpose(bank[2 + t][:, j * P:(j + 1) * P], tok_kv[:, t, c:c + P], ident)
                                tr.then_inc(s_kvt, 1)
                            for n in range(4):
                                t, h = n // 2, n % 2
                                if n >= 2:
                                    pe.wait_ge(s_qtev, n - 1)
                                for j in range(4):
                                    c = (4 * h + j) * P
                                    tr = PE.transpose(bank[4 + h][:, j * P:(j + 1) * P], tok_q[:, t, c:c + P], ident)
                                tr.then_inc(s_qt, 1)
                            pe.wait_ge(s_kvtev, 2)
                            pe_col = vec("pe")
                            for u in UNSPLIT:
                                j, half = divmod(u - UNSPLIT.start, 2)
                                arrived(pe, u)
                                w1 = ring[:, u % RING].rearrange("p (l c) -> p l c", l=8)
                                o = bank[7][0:CROWS, j * S:(j + 1) * S]
                                for r in range(8):
                                    q = 8 * half + r
                                    PE.matmul(o, blocks[:, j, 2 * q:2 * q + 16 * (CROWS - 1) + 1:16], w1[:, r, :],
                                              start=(q == 0), stop=False)
                                    mm = PE.matmul(o, pe_col[:, 16 * j + q:16 * j + q + 1].to_broadcast([P, CROWS]), w1[:, r, :],
                                                   start=False, stop=(q == 15))
                                mm.then_inc(s_proj, 1)
                            PE.matmul(bank[6][0:1, 0:1], ident[:, 0:1], ident[:, 0:1], start=True, stop=True).then_inc(s_ch, 1)
                            gates(0)
                            pe.wait_ge(s_chg, 1)
                            for j in range(4):
                                tr = PE.transpose(bank[7][:, j * CROWS:(j + 1) * CROWS], chid[:, j * P:(j + 1) * P], ident[0:CROWS, 0:CROWS])
                            tr.then_inc(s_cht, 1)
                            gates(1)
                            pe.wait_ge(s_chtev, 1)
                            for j in range(2):
                                for g in range(G):
                                    for k in range(2):
                                        mm = PE.matmul(bank[6][0:NCMP, (2 * j + g) * DH:(2 * j + g + 1) * DH],
                                                       chT[:, 2 * j + k, g * 16:g * 16 + NCMP], w2[:, j, k, :],
                                                       start=(k == 0), stop=(k == 1))
                            mm.then_inc(s_co, 1)
                            gates(2)
                            pe.wait_ge(s_ckn, 1)
                            PE.transpose(bank[7][:, 0:NCMP], ck[:], ident[0:NCMP, 0:NCMP]).then_inc(s_ckt, 1)
                            pe.wait_ge(s_qtev, 4)
                            pe.wait_ge(s_cktev, 1)

                            def cmp_scores(t):
                                if t:
                                    pe.wait_ge(s_sctk, 2 * NP)
                                    pe.wait_ge(s_yev, 2)
                                for i in range(NP):
                                    for g in range(G):
                                        mm = PE.matmul(bank[2 + g][:, i * 16:i * 16 + NCMP], qT[g * DH:(g + 1) * DH, i, t * P:(t + 1) * P],
                                                       kcmpT[g * DH:(g + 1) * DH, :], start=True, stop=True)
                                mm.then_inc(s_cs, 1)

                            def scores(n):
                                t, i = units[n]
                                nk = (t + 1) * P
                                if i == 0:
                                    pe.wait_ge(s_cmask, 2 * t + 2)
                                elif n:
                                    pe.wait_ge(s_sctk, 2 * n)
                                for g in range(G):
                                    for b in range(2):
                                        mm = PE.matmul(bank[2 + g][:, b * nk:(b + 1) * nk],
                                                       qT[g * DH:(g + 1) * DH, i, t * P:(t + 1) * P],
                                                       kT[g * DH:(g + 1) * DH, b, 0:nk], start=True, stop=True)
                                mm.then_inc(s_sc, 1)

                            def turn(n):
                                t, i = units[n]
                                pe.wait_ge(s_scaled, n + 1)
                                pe.wait_ge(s_cp, t + 1)
                                if n:
                                    pe.wait_ge(s_ptev_a, 2 * n)
                                if n > NP:
                                    pe.wait_ge(s_ptev_v, n - NP)
                                for k in range(t + 1):
                                    for j in range(4):
                                        PE.transpose(bank[4 + k][:, j * P:(j + 1) * P], sc[:, n % 2, j, k * P:(k + 1) * P], ident)
                                for g in range(G):
                                    tr = PE.transpose(bank[7][0:NCMP, g * P:(g + 1) * P], pc[:, 2 * i + g, 0:NCMP], ident)
                                tr.then_inc(s_pt, 1)

                            def attend(n):
                                t, i = units[n]
                                pe.wait_ge(s_ptev_a, 2 * (n + 1))
                                if t:
                                    pe.wait_ge(s_ptev_v, n - NP + 1)
                                if n % 4 == 0 and n:
                                    pe.wait_ge(s_yev, n // 4)
                                for g in range(G):
                                    o = bank[6][g * DH:(g + 1) * DH, (n % 4) * P:(n % 4 + 1) * P]
                                    first_one = True
                                    for b, c in enumerate((VS, VW)):
                                        for k in range(t + 1):
                                            PE.matmul(o, tok_kv[:, k, c + g * DH:c + (g + 1) * DH],
                                                      pT[:, n % 2, k, (2 * g + b) * P:(2 * g + b + 1) * P],
                                                      start=first_one, stop=False)
                                            first_one = False
                                    mm = PE.matmul(o, vcmp[:, g * DH:(g + 1) * DH], pcT[:, n % 2, g * P:(g + 1) * P],
                                                   start=False, stop=True)
                                mm.then_inc(s_y, 1)

                            cmp_scores(0)
                            scores(0)
                            scores(1)
                            for n in range(1, len(units) + 1):
                                turn(n - 1)
                                if n + 1 < len(units) and n not in (NP - 1, NP):
                                    scores(n + 1)
                                gates(n + 2)
                                attend(n - 1)
                                if n == NP:
                                    cmp_scores(1)
                                    scores(n)
                                    scores(n + 1)

                            def branch_half(j):
                                n, f = divmod(j, 2)
                                if f == 0:
                                    if n % 4 == 0:
                                        pe.wait_ge(s_y1, n // 4 + 1)
                                    if n >= 2:
                                        pe.wait_ge(s_evac, EV0 + n - 1)
                                    if n == 1:
                                        pe.wait_ge(s_cbm, 1)
                                mm = feature_half(pe, BU + n, f, (feat, (lgH, lgL))[n // 4],
                                                  bank[6 + n % 2][:, f * S:(f + 1) * S])
                                if f:
                                    mm.then_inc(s_proj, 1)

                            pe.wait_ge(s_yev, 4)
                            for c in range(NT):
                                PE.matmul(bank[7][:, 2 * c * SH:(2 * c + 1) * SH], upper, adt[:, c, :], start=True, stop=True)
                                mm = PE.matmul(bank[7][:, (2 * c + 1) * SH:(2 * c + 2) * SH], strict, adt[:, c, :],
                                               start=True, stop=True)
                            mm.then_inc(s_sd, 1)
                            for n in range(4):
                                c, h = n // 2, n % 2
                                if n >= 2:
                                    pe.wait_ge(s_xtev, n - 1)
                                for j in range(4):
                                    tr = PE.transpose(bank[4 + h][:, j * P:(j + 1) * P],
                                                      xbcC[:, 4 * h + j, c * P:(c + 1) * P], ident)
                                tr.then_inc(s_xt, 1)
                            for g in range(G):
                                tr = PE.transpose(bank[6][:, g * P:(g + 1) * P], xbcC[:, 8 + g, 0:P], ident)
                            tr.then_inc(s_xt, 1)
                            pe.wait_ge(s_sde, 1)
                            for c in range(NT):
                                for g in range(G):
                                    mm = PE.matmul(bank[7][:, (2 * c + g) * P:(2 * c + g + 1) * P],
                                                   xbcC[:, 8 + g, c * P:(c + 1) * P], xbcC[:, 10 + g, c * P:(c + 1) * P],
                                                   start=True, stop=True)
                            mm.then_inc(s_cb, 1)
                            pe.wait_ge(s_xtev, 5)
                            pe.wait_ge(s_xd, 2)
                            for g in range(G):
                                PE.matmul(bank[g][:], b_tok[:, g, :], xdec[:, g * 512:(g + 1) * 512],
                                          start=True, stop=True).then_inc(s_s0, 1)

                            def segsum(n):
                                pe.wait_ge(s_au, n + 1)
                                if n >= 2:
                                    pe.wait_ge(s_dec, n - 1)
                                PE.matmul(bank[2 + n % 2][:], strict, au[:, n % 2].rearrange("p h l -> p (h l)"),
                                          start=True, stop=True).then_inc(s_seg, 1)

                            def ssd_y(n):
                                c, q = n // 4, n % 4
                                g = q // 2
                                pe.wait_ge(s_m, n + 1)
                                if q % 2 == 0 and 2 * c + g >= 2:
                                    pe.wait_ge(s_ydtk, 2 * c + g - 1)
                                for j in range(4):
                                    h = 4 * q + j
                                    mm = PE.matmul(bank[4 + g][:, (h % 8) * DH:(h % 8 + 1) * DH], dec[:, n % 2, j, :],
                                                   xdt[:, c, h * DH:(h + 1) * DH], start=True, stop=True)
                                mm.then_inc(s_yd, 1)

                            for n in range(9):
                                if n < 8:
                                    segsum(n)
                                    branch_half(n)
                                if n:
                                    ssd_y(n - 1)
                            pe.wait_ge(s_s0ev, 2)
                            for g in range(G):
                                PE.matmul(bank[g][:], xbcC[:, 10 + g, P:S], s0[:, g, :], start=True, stop=True).then_inc(s_yo, 1)
                            for j in range(8, 14):
                                branch_half(j)
                            pe.wait_ge(s_dec, 8)
                            for n in range(4):
                                t, h = n // 2, n % 2
                                pe.wait_ge(s_zn, n + 1)
                                if n >= 2:
                                    pe.wait_ge(s_ztev, n - 1)
                                for j in range(4):
                                    tr = PE.transpose(bank[2 + h][:, j * P:(j + 1) * P],
                                                      tok_z[:, t, (4 * h + j) * P:(4 * h + j + 1) * P], ident)
                                tr.then_inc(s_zt, 1)
                                if n == 1:
                                    branch_half(14)
                                    branch_half(15)

                        @block.scalar
                        def _(act):
                            def take_gates(n):
                                if n < NMG:
                                    act.wait_ge(s_proj, MGU + n + 1)
                                    A.activation(mgT[:, 2 * n:2 * n + 2, :],
                                                 bank[n % 2][:].rearrange("p (f s) -> p f s", f=2), ACT.Copy).then_inc(s_evac, 1)
                                    if n + HIS < NMG:
                                        split_hi(act, MGU + n + HIS)

                            A.activation(gsig[:], tok_kv[:, :, GATE:GATE + 48], ACT.Sigmoid).then_inc(s_sig, 1)
                            for t in range(NT):
                                act.wait_ge(s_kvt, t + 1)
                                for j, c in enumerate((0, 3)):
                                    for g in range(G):
                                        src = bank[2 + t][g * DH:(g + 1) * DH, c * P:(c + 1) * P]
                                        A.activation(cT[0:DH, j, g, t * P:(t + 1) * P], src, ACT.Copy)
                                        if t == 0:
                                            A.activation(cT[DH:P, j, g, 0:P - 1], src[:, 1:P], ACT.Copy)
                                        else:
                                            A.activation(cT[DH:P, j, g, P - 1:S - 1], src, ACT.Copy)
                                A.activation(kT[:, :, t * P:(t + 1) * P],
                                             bank[2 + t][:, P:3 * P].rearrange("p (b s) -> p b s", b=2),
                                             ACT.Copy).then_inc(s_kvtev, 1)
                            for n in range(HIS):
                                split_hi(act, MGU + n)
                            act.wait_ge(s_ch, 1)
                            A.activation(chid[:], bank[7][0:CROWS, :], ACT.Gelu_apprx_tanh).then_inc(s_chg, 1)
                            take_gates(0)
                            act.wait_ge(s_cht, 1)
                            A.activation(chT[:], bank[7][:, 0:4 * CROWS].rearrange("p (j c) -> p j c", j=4), ACT.Copy).then_inc(s_chtev, 1)
                            take_gates(1)
                            act.wait_ge(s_cksq, 1)
                            A.activation(kst[:, 0:2], kst[:, 0:2], ACT.Sqrt, scale=1 / DH).then_inc(s_ckrt, 1)
                            take_gates(2)
                            act.wait_ge(s_ckt, 1)
                            A.activation(kcmpT[:], bank[7][:, 0:NCMP], ACT.Copy).then_inc(s_cktev, 1)

                            def exps(n):
                                t, i = units[n]
                                nk = (t + 1) * P
                                act.wait_ge(s_max, n + 1)
                                for j in range(4):
                                    e = A.activation(sc[:, n % 2, j, 0:nk], sc[:, n % 2, j, 0:nk], ACT.Exp,
                                                     bias=rst[:, n % 2, 0, j:j + 1], accum_out=rst[:, n % 2, 1, j:j + 1])
                                e.then_inc(s_exp, 1)

                            def take_turned(n):
                                act.wait_ge(s_pt, n + 1)
                                if n >= 2:
                                    act.wait_ge(s_y, n - 1)
                                A.activation(pT[:, n % 2, 0, :], bank[4][:], ACT.Copy).then_inc(s_ptev_a, 1)
                                A.activation(pcT[:, n % 2, :], bank[7][0:NCMP, 0:2 * P], ACT.Copy).then_inc(s_ptev_a, 1)

                            def cmp_exp(t):
                                act.wait_ge(s_cand, t + 1)
                                A.activation(pc[:, :, 0:NCMP], pc[:, :, 0:NCMP], ACT.Exp).then_inc(s_cexp, 1)

                            for n in range(len(units) + 1):
                                if n == 0:
                                    cmp_exp(0)
                                if n == NP:
                                    take_turned(n - 1)
                                    take_gates(n + 2)
                                    cmp_exp(1)
                                    exps(n)
                                    continue
                                if n < len(units):
                                    exps(n)
                                if n:
                                    take_turned(n - 1)
                                    take_gates(n + 2)

                            act.wait_ge(s_proj, MGU + NMG)
                            act.wait_ge(s_yev, 4)
                            act.wait_ge(s_sd, 1)
                            A.activation(ssd_e[:], bank[7][:, 0:4 * SH].rearrange("p (c h) -> p c h", c=NT), ACT.Exp).then_inc(s_sde, 1)
                            for n in range(4):
                                c, h = n // 2, n % 2
                                act.wait_ge(s_xt, n + 1)
                                A.activation(xs_tok[:, c, h * 512:(h + 1) * 512], bank[4 + h][:], ACT.Copy).then_inc(s_xtev, 1)
                            act.wait_ge(s_xt, 5)
                            A.activation(b_tok[:], bank[6][:, 0:2 * P].rearrange("p (g n) -> p g n", g=G), ACT.Copy).then_inc(s_xtev, 1)
                            A.activation(featH[:], yaT, ACT.Copy).then_inc(s_y0, 1)
                            split_hi(act, BU)
                            split_hi(act, BU + 1)
                            for b in range(2):
                                A.activation(mgT[:, 8 * b:8 * b + 8, :], mgT[:, 8 * b:8 * b + 8, :], ACT.Sigmoid).then_inc(s_mgs, 1)
                            for g in range(G):
                                act.wait_ge(s_s0, g + 1)
                                A.activation(s0[:, g, :], bank[g][:], ACT.Copy).then_inc(s_s0ev, 1)
                            for n in range(8):
                                act.wait_ge(s_seg, n + 1)
                                if n >= 2:
                                    act.wait_ge(s_yd, n - 1)
                                A.activation(dec[:, n % 2].rearrange("p h l -> p (h l)"), bank[2 + n % 2][:], ACT.Exp).then_inc(s_dec, 1)
                                if n == 3:
                                    act.wait_ge(s_y1, 1)
                                    A.activation(lgH[:], lgT[:], ACT.Copy).then_inc(s_y0, 1)
                                if n % 2 == 0:
                                    split_hi(act, BU + 2 + n // 2)
                            split_hi(act, BU + 6)
                            for n in range(4):
                                t, h = n // 2, n % 2
                                act.wait_ge(s_zy, n + 1)
                                ach.link(A.activation(zsq[:], tok_z[:, t, h * 512:(h + 1) * 512], ACT.Square,
                                                      accum_out=st[:, 8 + n:9 + n]))
                                A.activation(st[:, 12 + n:13 + n], st[:, 8 + n:9 + n], ACT.Sqrt, bias=eps[:],
                                             scale=2 / D).then_inc(s_zrt, 1)
                                if n == 1:
                                    split_hi(act, BU + 7)
                            A.activation(mgT[:, 16:24, :], mgT[:, 16:24, :], ACT.Sigmoid).then_inc(s_mgs, 1)
                            for n in range(8, 8 + HIS):
                                split_hi(act, BU + n)
                            act.wait_ge(s_mgs, 3)

                        @block.gpsimd
                        def _(pool):
                            for n in range(4):
                                split_lo(pool, MGU + n)
                            for n in range(len(units)):
                                t, i = units[n]
                                nk = (t + 1) * P
                                pool.wait_ge(s_coef, n + 1)
                                PO.tensor_tensor(sc[:, n % 2, :, 0:nk], sc[:, n % 2, :, 0:nk],
                                                 over(rst[:, n % 2, 2, :], nk), ALU.mult).then_inc(s_scaled, 1)
                                if n + 4 < NMG:
                                    split_lo(pool, MGU + n + 4)
                            def adt_upper(n):
                                c, q = n // 4, n % 4
                                if n >= 2:
                                    pool.wait_ge(s_seg, n - 1)
                                else:
                                    pool.wait_ge(s_pt, len(units))
                                PO.tensor_tensor(au[:, n % 2], times(upper, 4), over(adt[:, c, 4 * q:4 * q + 4], P),
                                                 ALU.mult).then_inc(s_au, 1)

                            adt_upper(0)
                            adt_upper(1)
                            pool.wait_ge(s_yev, 4)
                            pool.wait_ge(s_proj, MGU + NMG)
                            pool.wait_ge(s_y0, 1)
                            PO.tensor_tensor(featL[:], yaT, featH[:].bitcast(F32), ALU.subtract).then_inc(s_y1, 1)
                            split_lo(pool, BU)
                            adt_upper(2)
                            adt_upper(3)
                            split_lo(pool, BU + 2)
                            adt_upper(4)
                            pool.wait_ge(s_y0, 2)
                            PO.tensor_tensor(lgL[:], lgT[:], lgH[:].bitcast(F32), ALU.subtract).then_inc(s_y1, 1)
                            adt_upper(5)
                            split_lo(pool, BU + 4)
                            adt_upper(6)
                            adt_upper(7)
                            for n in (6, 8, 10):
                                split_lo(pool, BU + n)

                        @block.vector
                        def _(dve):
                            for n in range(4):
                                t, h = n // 2, n % 2
                                dve.wait_ge(s_qt, n + 1)
                                V.tensor_copy(qT[:, 4 * h:4 * h + 4, t * P:(t + 1) * P],
                                              bank[4 + h][:].rearrange("p (f s) -> p f s", f=4)).then_inc(s_qtev, 1)
                            dve.wait_ge(s_co, 1)
                            dch.add(V.tensor_copy(vcmp[:], bank[6][0:NCMP, P:2 * P]))
                            dch.link(V.tensor_copy(ck[:], bank[6][0:NCMP, 0:P]))
                            ckv = ck.rearrange("p (g d) -> p g d", g=G)
                            sqv = cksq.rearrange("p (g d) -> p g d", g=G)
                            dch.link(V.tensor_tensor(cksq[:], ck[:], ck[:], ALU.mult))
                            dch.link(V.tensor_reduce(kst[:, 0:2], sqv, AX, ALU.add))
                            V.tensor_scalar(kst[:, 0:2], kst[:, 0:2], DH * EPS, None, ALU.add).then_inc(s_cksq, 1)
                            dve.wait_ge(s_ckrt, 1)
                            dch.link(V.reciprocal(kst[:, 2:4], kst[:, 0:2]))
                            dch.link(V.tensor_tensor(ckv, ckv, over(kst[:, 2:4], DH), ALU.mult))
                            V.tensor_tensor(ckv, ckv, times(row[0:NCMP, ROW_KG:ROW_KG + DH], G), ALU.mult).then_inc(s_ckn, 1)

                            pcv = pc[:, :, 0:NCMP]

                            def cmp_max(t):
                                dve.wait_ge(s_cs, t + 1)
                                if t:
                                    dve.wait_ge(s_pt, NP)
                                pg = pc.rearrange("p (i g) c -> p i g c", g=G)
                                for g in range(G):
                                    V.scalar_tensor_tensor(pg[:, :, g, 0:NCMP],
                                                           bank[2 + g][:, 0:P].rearrange("p (i c) -> p i c", i=NP)[:, :, 0:NCMP],
                                                           SCALE, times(cst[:, C_CMPB + 16 * t:C_CMPB + 16 * t + NCMP], NP),
                                                           ALU.mult, ALU.add).then_inc(s_cmask, 1)
                                dve.wait_ge(s_cmask, 2 * t + 2)
                                dch.link(V.tensor_reduce(cst2[:, 0, :], pcv, AX, ALU.max))
                                V.tensor_tensor(pcv, pcv, over(cst2[:, 0, :], NCMP), ALU.subtract).then_inc(s_cand, 1)

                            def cmp_probs(t):
                                dve.wait_ge(s_cexp, t + 1)
                                dch.link(V.tensor_reduce(cst2[:, 1, :], pcv, AX, ALU.add))
                                dch.link(V.reciprocal(cst2[:, 1, :], cst2[:, 1, :]))
                                dch.link(V.tensor_tensor(cst2[:, 2, :], cst2[:, 1, :],
                                                         gsig[:, t, :].rearrange("p (h b) -> p h b", b=3)[:, :, 0], ALU.mult))
                                dch.link(V.tensor_tensor(pcv, pcv, over(cst2[:, 2, :], NCMP), ALU.mult))
                                V.tensor_tensor(pcv, pcv, times(cst[:, C_CMPM + 16 * t:C_CMPM + 16 * t + NCMP], 2 * NP),
                                                ALU.mult).then_inc(s_cp, 1)

                            def row_max(n):
                                t, i = units[n]
                                nk = (t + 1) * P
                                dve.wait_ge(s_sc, n + 1)
                                if n >= 2:
                                    dve.wait_ge(s_pt, n - 1)
                                mask = cst[:, C_CAUSAL + P:C_CAUSAL + 2 * P] if t == 0 else cst[:, C_CAUSAL:C_CAUSAL + 2 * P]
                                for g in range(G):
                                    V.scalar_tensor_tensor(sc[:, n % 2, 2 * g:2 * g + 2, 0:nk],
                                                           bank[2 + g][:, 0:2 * nk].rearrange("p (b k) -> p b k", b=2),
                                                           SCALE, times(mask, 2), ALU.mult, ALU.add).then_inc(s_sctk, 1)
                                dve.wait_ge(s_sctk, 2 * n + 2)
                                V.tensor_reduce(rst[:, n % 2, 0, :], sc[:, n % 2, :, 0:nk], AX, ALU.max,
                                                negate=True).then_inc(s_max, 1)

                            def coefficients(n):
                                t, i = units[n]
                                dve.wait_ge(s_exp, n + 1)
                                dch.link(V.reciprocal(rst[:, n % 2, 1, :], rst[:, n % 2, 1, :]))
                                V.tensor_tensor(rst[:, n % 2, 2, :].rearrange("p (g b) -> p g b", g=G),
                                                rst[:, n % 2, 1, :].rearrange("p (g b) -> p g b", g=G),
                                                gsig[:, t, :].rearrange("p (h b) -> p h b", b=3)[:, 2 * i:2 * i + 2, 1:3],
                                                ALU.mult).then_inc(s_coef, 1)

                            def take_turned(n):
                                t, i = units[n]
                                if t:
                                    dve.wait_ge(s_pt, n + 1)
                                    dve.wait_ge(s_y, n - 1)
                                    V.tensor_copy(pT[:, n % 2, 1, :], bank[5][:]).then_inc(s_ptev_v, 1)

                            def take_y(n):
                                if n % 4 == 3:
                                    t, q = n // 8, (n // 4) % 2
                                    dve.wait_ge(s_y, n + 1)
                                    V.tensor_copy(yaT[:, 4 * q:4 * q + 4, t * P:(t + 1) * P],
                                                  bank[6][:].rearrange("p (i s) -> p i s", i=4)).then_inc(s_yev, 1)

                            dve.wait_ge(s_sig, 1)
                            cmp_max(0)
                            cmp_probs(0)
                            row_max(0)
                            for n in range(1, len(units) + 1):
                                coefficients(n - 1)
                                if n < len(units) and n != NP:
                                    row_max(n)
                                take_turned(n - 1)
                                take_y(n - 1)
                                if n == NP:
                                    cmp_max(1)
                                    cmp_probs(1)
                                    row_max(n)

                            dve.wait_ge(s_xtev, 4)
                            dve.wait_ge(s_sde, 1)
                            xh = [xs_tok[:, c, :].rearrange("p (h d) -> p h d", h=SH) for c in range(NT)]
                            for c in range(NT):
                                dch.add(V.tensor_tensor(xdt[:, c, :].rearrange("p (h d) -> p h d", h=SH), xh[c],
                                                        over(dt[:, c, :], DH), ALU.mult))
                            dch.settle()
                            dve.sem_inc(s_xd, 1)
                            V.tensor_tensor(xdec.rearrange("p (h d) -> p h d", h=SH),
                                            xdt[:, 0, :].rearrange("p (h d) -> p h d", h=SH),
                                            over(ssd_e[:, 0, SH:2 * SH], DH), ALU.mult).then_inc(s_xd, 1)
                            dve.wait_ge(s_cb, 1)
                            V.tensor_tensor(cbm.rearrange("p c g l -> p (c g) l"),
                                            bank[7][:].rearrange("p (n l) -> p n l", n=4), times(upper, 4), ALU.mult
                                            ).then_inc(s_cbm, 1)
                            dve.wait_ge(s_cbm, 1)

                            def gate_branch(n):
                                dve.wait_ge(s_proj, BU + n + 1)
                                dve.wait_ge(s_mgs, n // 4 + 1)
                                g = mgT[:, 2 * n:2 * n + 2, :]
                                V.tensor_tensor(g, g, bank[6 + n % 2][:].rearrange("p (f s) -> p f s", f=2), ALU.mult).then_inc(s_evac, 1)

                            def decayed(n):
                                c, q = n // 4, n % 4
                                dve.wait_ge(s_dec, n + 1)
                                V.tensor_tensor(dec[:, n % 2], dec[:, n % 2], times(cbm[:, c, q // 2, :], 4), ALU.mult).then_inc(s_m, 1)

                            def gated(c, g):
                                n = 2 * c + g
                                yh = yt.rearrange("p (h d) -> p h d", h=8)
                                dch.link(V.tensor_tensor(yh, xh[c][:, 8 * g:8 * g + 8, :],
                                                         over(row[:, ROW_D + 8 * g:ROW_D + 8 * g + 8], DH), ALU.mult))
                                dve.wait_ge(s_yd, 4 * c + 2 * g + 2)
                                V.tensor_tensor(yt, yt, bank[4 + g][:], ALU.add).then_inc(s_ydtk, 1)
                                dve.wait_ge(s_ydtk, n + 1)
                                if c:
                                    dve.wait_ge(s_yo, g + 1)
                                    dch.link(V.tensor_tensor(yt2.rearrange("p (h d) -> p h d", h=8),
                                                             bank[g][:].rearrange("p (h d) -> p h d", h=8),
                                                             over(ssd_e[:, 1, 8 * g:8 * g + 8], DH), ALU.mult))
                                    dch.link(V.tensor_tensor(yt, yt, yt2, ALU.add))
                                z = tok_z[:, c, g * 512:(g + 1) * 512]
                                V.tensor_tensor(z, z, yt, ALU.mult).then_inc(s_zy, 1)
                                dve.wait_ge(s_zy, n + 1)

                            def normed_z(n):
                                t, h = n // 2, n % 2
                                dve.wait_ge(s_zrt, n + 1)
                                dch.link(V.reciprocal(st[:, 16 + n:17 + n], st[:, 12 + n:13 + n]))
                                z = tok_z[:, t, h * 512:(h + 1) * 512]
                                V.tensor_scalar(z, z, st[:, 16 + n:17 + n], None, ALU.mult).then_inc(s_zn, 1)

                            split_lo(dve, BU + 1)
                            for n in range(4):
                                decayed(n)
                                if n % 2:
                                    gate_branch(n // 2)
                                elif n == 2:
                                    split_lo(dve, BU + 3)
                            gated(0, 0)
                            gated(0, 1)
                            for n in range(4, 8):
                                decayed(n)
                                if n % 2:
                                    gate_branch(n // 2)
                                if n == 6:
                                    split_lo(dve, BU + 5)
                            gated(1, 0)
                            gate_branch(4)
                            gated(1, 1)
                            gate_branch(5)
                            split_lo(dve, BU + 7)
                            for n in range(4):
                                normed_z(n)
                                if n % 2:
                                    gate_branch(6 + n // 2)
                            for n in range(4):
                                t, h = n // 2, n % 2
                                at = (slice(None), slice(4 * h, 4 * h + 4), slice(t * P, (t + 1) * P))
                                dve.wait_ge(s_zt, n + 1)
                                V.tensor_tensor(ycT[at], bank[2 + h][:].rearrange("p (f s) -> p f s", f=4),
                                                over(vec("ssm_g")[:, 4 * h:4 * h + 4], P), ALU.mult).then_inc(s_ztev, 1)
                                dve.wait_ge(s_ztev, n + 1)
                                dch.link(V.tensor_copy(featH[at], ycT[at]))
                                dch.add(V.tensor_tensor(featL[at], ycT[at], featH[at].bitcast(F32), ALU.subtract))
                            split_lo(dve, BU + 9)
                            dch.settle()

                early.close()
                OU = 2 * OUT0
                opH, opL = sb("opH", [P, KT, S], F32R, mix), sb("opL", [P, KT, S], F32R, mix)
                merged = mgT[:, 0:KT, :]
                op = (opH, opL)
                with nc.Block(no_gpsimd_drain=True) as block:
                    @block.sync
                    def _(sp):
                        for u in range(BU + 8 + RING, 2 * PQ0 + RING):
                            load(sp, u)

                    @block.tensor
                    def _(pe):
                        for n in range(8, 12):
                            feature_unit(pe, BU + n, feat, 4)
                        pe.wait_ge(s_y1, 3)
                        for n in range(4):
                            pe.wait_ge(s_evac, EV0 + 12 + n - 3)
                            token_unit(pe, OU + n, op, 4)

                    @block.scalar
                    def _(act):
                        for n in range(8, 16):
                            split_hi(act, BU + n + HIS)

                    @block.vector
                    def _(dve):
                        for n in range(8, 12):
                            q = n % 4
                            dst, second, third = (mgT[:, 8 * b + 2 * q:8 * b + 2 * q + 2, :] for b in range(3))
                            dch.link(V.tensor_tensor(dst, dst, second, ALU.add))
                            dve.wait_ge(s_proj, BU + n + 1)
                            src = bank[(BU + n) % 4][:].rearrange("p (f s) -> p f s", f=2)
                            V.tensor_tensor(third, third, src, ALU.mult).then_inc(s_evac, 1)
                            dve.wait_ge(s_evac, EV0 + n + 1)
                            dch.link(V.tensor_tensor(dst, dst, third, ALU.add))
                            dch.link(V.tensor_copy(opH[:, 2 * q:2 * q + 2, :], dst))
                            dch.add(V.tensor_tensor(opL[:, 2 * q:2 * q + 2, :], dst,
                                                    opH[:, 2 * q:2 * q + 2, :].bitcast(F32), ALU.subtract))
                            split_lo(dve, BU + n + HIS)
                        dch.settle()
                        dve.sem_inc(s_y1, 1)
                        for n in range(4):
                            dve.wait_ge(s_proj, OU + n + 1)
                            xv = x[:, :, n * 256:(n + 1) * 256]
                            V.tensor_tensor(xv, xv, bank[(OU + n) % 4][:].rearrange("p (t c) -> p t c", t=NT),
                                            ALU.add).then_inc(s_evac, 1)
                            split_lo(dve, OU + n + HIS)
                        dve.wait_ge(s_evac, EV0 + 16)

            late_at = layer_at + EXPERT_SMALL + 4 * EARLY * S
            key_at = layer_at + EXPERT_SMALL + 4 * NKEY * S - 4 * NT * 16 * P
            s_key = nc.alloc_sbuf_tensor_at("s_key", [P, NT, 16, P], F32, offset=key_at)
            xr_hi = nc.alloc_sbuf_tensor_at("xr_hi", [P, XR, D], F32R, offset=layer_at)
            xr = nc.alloc_sbuf_tensor_at("xr", [P, XR, D], F32, offset=layer_at + 4 * XR * D)
            xr_lo = nc.alloc_sbuf_tensor_at("xr_lo", [P, XR, D], F32R, offset=layer_at + 4 * XR * D)
            assert (PIECES - 4) % RING == 2 and 2 * XR * D == RING * WCOL

            def x_load(sp, m):
                if m >= XR:
                    sp.wait_ge(s_xu, m - XR + 1)
                else:
                    sp.wait_ge(s_proj, PIECES - 4 + m // 2 + 1)
                sp.dma_start(xr[:, m % XR], xstream[bass.ds(layer * (2 * NKEY) + m, 1)].rearrange("a p c -> (a p) c")
                             ).then_inc(s_xl[m % XR], 16)

            def x_hi(act, m):
                if m >= 2 * NKEY:
                    return
                act.wait_ge(s_xl[m % XR], 16 * (m // XR + 1))
                if m >= XR:
                    act.wait_ge(s_xu, m - XR + 1)
                A.activation(xr_hi[:, m % XR], xr[:, m % XR], ACT.Copy).then_inc(s_xhi, 1)

            def x_lo(eng, m):
                eng.wait_ge(s_xhi, m + 1)
                (PO if m < NKEY else V).tensor_tensor(
                    xr_lo[:, m % XR], xr[:, m % XR], xr_hi[:, m % XR].bitcast(F32), ALU.subtract
                ).then_inc(s_xlo_pool if m < NKEY else s_xlo_dve, 1)

            ffn = ExitStack()
            with ffn:
                h_tok = sb("h_tok", [P, NT, D], F32, ffn)
                subk = sb("subk", [P, 16, P], F32, ffn)
                QU = 2 * PQ0
                EV1 = 26 + 12 + 16
                with ExitStack() as tmp:
                    qpT = sb("qpT", [P, 16, S], F32, tmp)
                    g_row = sb("g_row", [P, D], F32, tmp)
                    sq = sb("sq", [P, D], F32, tmp)
                    with nc.Block(no_gpsimd_drain=True) as block:
                        @block.sync
                        def _(sp):
                            sp.dma_start(g_row[:], ffn_row[bass.ds(layer, 1)].rearrange("a c -> (a c)").partition_broadcast(P)
                                         ).then_inc(s_hrow, 16)
                            sp.dma_start(subk[:], subkeys[bass.ds(layer, 1)].rearrange("a p c k -> (a p) c k")
                                         ).then_inc(s_subk, 16)
                            for u in range(2 * PQ0 + RING, PIECES):
                                load(sp, u)
                            for m in range(XR):
                                x_load(sp, m)

                        @block.scalar
                        def _(act):
                            for t in range(NT):
                                ach.link(A.activation(sq[:], x[:, t, :], ACT.Square, accum_out=st[:, t:t + 1]))
                            A.activation(st[:, 2:4], st[:, 0:2], ACT.Sqrt, bias=eps[:], scale=1 / D).then_inc(s_hrt, 1)
                            for n in range(8):
                                act.wait_ge(s_proj, QU + n + 1)
                                A.activation(qpT[:, 2 * n:2 * n + 2, :],
                                             bank[(QU + n) % 4][:].rearrange("p (f s) -> p f s", f=2), ACT.Copy).then_inc(s_evac, 1)
                                split_hi(act, QU + n + HIS)
                            for n in range(8):
                                act.wait_ge(s_ps, n + 1)
                                A.activation(s_key[:, n // 4, 4 * (n % 4):4 * (n % 4) + 4, :],
                                             bank[4 + n % 2][:].rearrange("p (f s) -> p f s", f=4), ACT.Copy).then_inc(s_psev, 1)
                            act.wait_ge(s_proj, PIECES)
                            for m in range(XR - 1):
                                x_hi(act, m)
                            act.wait_ge(s_psev, 8)

                        @block.gpsimd
                        def _(pool):
                            for m in range(XR - 1):
                                x_lo(pool, m)

                        @block.vector
                        def _(dve):
                            dve.wait_ge(s_hrt, 1)
                            dve.wait_ge(s_hrow, 16)
                            dch.link(V.reciprocal(st[:, 4:6], st[:, 2:4]))
                            for t in range(NT):
                                V.scalar_tensor_tensor(h_tok[:, t, :], x[:, t, :], st[:, 4 + t:5 + t], g_row[:],
                                                       ALU.mult, ALU.mult).then_inc(s_hn, 1)
                            for n in range(4):
                                t, h = n // 2, n % 2
                                dve.wait_ge(s_ht, n + 1)
                                at = (slice(None), slice(4 * h, 4 * h + 4), slice(t * P, (t + 1) * P))
                                ht = bank[6 + h][:].rearrange("p (f s) -> p f s", f=4)
                                dch.link(V.tensor_copy(featH[at], ht))
                                V.tensor_tensor(featL[at], ht, featH[at].bitcast(F32), ALU.subtract).then_inc(s_htev, 1)
                            for n in range(8):
                                split_lo(dve, QU + n + HIS)

                        @block.tensor
                        def _(pe):
                            for n in range(4):
                                t, h = n // 2, n % 2
                                pe.wait_ge(s_hn, t + 1)
                                if n >= 2:
                                    pe.wait_ge(s_htev, n - 1)
                                for j in range(4):
                                    tr = PE.transpose(bank[6 + h][:, j * P:(j + 1) * P],
                                                      h_tok[:, t, (4 * h + j) * P:(4 * h + j + 1) * P], ident)
                                tr.then_inc(s_ht, 1)
                            pe.wait_ge(s_htev, 4)
                            for n in range(8):
                                if n >= 4:
                                    pe.wait_ge(s_evac, EV1 + n - 3)
                                feature_unit(pe, QU + n, feat, 4)
                            pe.wait_ge(s_subk, 16)
                            pe.wait_ge(s_evac, EV1 + 8)
                            for n in range(8):
                                t = n // 4
                                if n >= 2:
                                    pe.wait_ge(s_psev, n - 1)
                                for j in range(4):
                                    hx = 4 * (n % 4) + j
                                    mm = PE.matmul(bank[4 + n % 2][:, j * P:(j + 1) * P], qpT[:, hx, t * P:(t + 1) * P],
                                                   subk[:, hx, :], start=True, stop=True)
                                mm.then_inc(s_ps, 1)

            wide.close()
            with ExitStack() as tmp:
                sb("expert_pieces", [P, 2 * XR * D], F32, tmp)
                pair_at = nc.sbuf_base
                gelu = sb("gelu", [P, 2, 2, S], F32, tmp)
                p_hi = nc.alloc_sbuf_tensor_at("p_hi", [P, 2, 2, S], F32R, offset=pair_at)
                hot = sb("hot", [P, 2, 2, GB, P], F32, tmp)
                choice = sb("choice", [P, 3, S], F32, tmp)
                acts_at = nc.sbuf_base
                assert acts_at + 4 * EARLY * S == late_at
                acts = sb("acts", [P, NKEY, S], F32, tmp)
                QUARTER = NKEY // 4
                acts_lo = [nc.alloc_sbuf_tensor_at(f"acts_lo_{q}", [P, QUARTER, S], F32R, offset=acts_at + 4 * q * QUARTER * S)
                           for q in range(4)]
                free_at = [late_at]

                def early_sb(name, shape, dt=F32):
                    t = nc.alloc_sbuf_tensor_at(name, [P] + shape, dt, offset=free_at[0])
                    free_at[0] += 4 * int(np.prod(shape))
                    assert free_at[0] <= key_at
                    return t

                cand = early_sb("cand", [PH, 256])
                place = early_sb("place", [STEPS, 16])
                top_v, top_iu, top_i = early_sb("top_v", [16, TOPK]), early_sb("top_iu", [16, TOPK], U32), early_sb("top_i", [16, TOPK])
                cut = early_sb("cut", [256])
                best, pos = early_sb("best", [PH, TOPK]), early_sb("pos", [PH, TOPK], U32)
                part, partf = early_sb("part", [STEPS], U32), early_sb("partf", [STEPS])
                sel = early_sb("sel", [NT, 3, STEPS])
                gs = early_sb("gs", [NT, 2, PH])
                GT = S // GB
                EVERY = 6
                GBANKS = 3
                UBANKS = 8 - GBANKS
                HELD = 2 * UBANKS
                LAG = 3
                VU = NKEY
                hot3 = nc.alloc_sbuf_tensor_at("hot3", [P, 2, GB, P], F32, offset=pair_at)

                def hots(g):
                    return (hot[:, 0], hot[:, 1], hot3[:])[g % 3]

                def held_after(g):
                    return g // EVERY if g >= 0 and g % EVERY == EVERY - 1 and g // EVERY < HELD else None

                def spread(g, c):
                    return (acts[:, c, GB * g:GB * (g + 1)],
                            bank[g % GBANKS][:].rearrange("p (s i) -> p i s", s=GB)[:, c, :])

                LATE_PAIRS = (NKEY - EARLY) // 2

                def pslot(r):
                    return (r + LATE_PAIRS) % 2

                def ubank(m):
                    return bank[GBANKS + (m // 2) % UBANKS]

                def gate_rows(t):
                    return sel[:, t, 2, :].rearrange("p (h k) -> p h k", h=PH)

                with nc.Block(no_gpsimd_drain=True) as block:
                    @block.sync
                    def _(sp):
                        for m in range(XR, 2 * NKEY):
                            x_load(sp, m)

                    @block.tensor
                    def _(pe):
                        def u_unit(m):
                            b = ubank(m)[:, (m % 2) * S:(m % 2 + 1) * S]
                            if m >= HELD and m % 2 == 0:
                                pe.wait_ge(s_uev, m // 2 - UBANKS + 1)
                            pe.wait_ge(s_xlo_pool, m + 1)
                            w = [a[:, m % XR].rearrange("p (k c) -> p k c", k=KT) for a in (xr_hi, xr_lo)]
                            for k in range(KT):
                                mm = three_passes(b, [a[:, k, :] for a in w], [a[:, k, :] for a in feat],
                                                  k == 0, k == KT - 1)
                            mm.then_inc(s_xu, 1)

                        for m in range(EARLY):
                            u_unit(m)
                            if m == EARLY - 2:
                                pe.wait_ge(s_chosen, 1)
                                for t in range(NT):
                                    for j in range(3):
                                        tr = PE.transpose(bank[t][:, j * P:(j + 1) * P], sel[:, t, j, :], ident)
                                    tr.then_inc(s_gt, 1)
                        for g in range(GT):
                            if g >= GBANKS:
                                pe.wait_ge(s_gev_a, g - GBANKS + 1)
                                pe.wait_ge(s_gev_v, g - GBANKS + 1)
                            pe.wait_ge(s_wp, g + 1)
                            pe.wait_ge(s_wa, g + 1)
                            for j in range(GB):
                                mm = PE.matmul(bank[g % GBANKS][:, j * P:(j + 1) * P], hots(g)[:, 0, j, :], hots(g)[:, 1, j, :],
                                               start=True, stop=True)
                            mm.then_inc(s_gates, 1)
                            if held_after(g) is not None:
                                u_unit(EARLY + held_after(g))
                        for m in range(EARLY + HELD, NKEY):
                            u_unit(m)
                        pe.wait_ge(s_gev_v, GT)
                        pe.wait_ge(s_gev_a, GT)
                        for i in range(NKEY):
                            pe.wait_ge(s_plo, i // 2 + 1)
                            pe.wait_ge(s_xlo_dve, i + 1)
                            m = VU + i
                            for t in range(NT):
                                ph = p_hi[:, pslot(i // 2), i % 2, t * P:(t + 1) * P]
                                pl = acts_lo[i // QUARTER][:, i % QUARTER, t * P:(t + 1) * P]
                                for p, w, first, last in ((ph, xr_hi, True, False), (ph, xr_lo, False, False), (pl, xr_hi, False, True)):
                                    for h in range(2):
                                        mm = PE.matmul(bank[2 * t + h][:], p, w[:, m % XR, h * 512:(h + 1) * 512],
                                                       start=first and i == 0, stop=last and i == NKEY - 1)
                            mm.then_inc(s_xu, 1)

                    @block.scalar
                    def _(act):
                        def activations(m, dst):
                            act.wait_ge(s_xu, m + 1)
                            A.activation(dst, ubank(m)[:].rearrange("p (i s) -> p i s", i=2),
                                         ACT.Gelu_apprx_tanh).then_inc(s_uev, 1)

                        for m in range(EARLY):
                            x_hi(act, m + XR - 1)
                            if m % 2:
                                activations(m, acts[:, m - 1:m + 1, :])
                            if m == EARLY - 3:
                                act.wait_ge(s_cand, 2 + NT + 1)
                                for t in range(NT):
                                    A.activation(gate_rows(t), gate_rows(t), ACT.Exp).then_inc(s_gexp, 1)
                        act.wait_ge(s_gttk, NT)
                        for g in range(GT + LAG):
                            if g < GT:
                                act.wait_ge(s_hot, g + 1)
                                h1, s = hots(g)[:, 0, GB - 1, :], GB * g + GB - 1
                                A.activation(h1, h1, ACT.Copy, scale=choice[:, 2, s:s + 1]).then_inc(s_wa, 1)
                            if g >= LAG:
                                act.wait_ge(s_gev_v, g - LAG + 1)
                                a, b = spread(g - LAG, slice(EARLY, NKEY))
                                A.activation(a, b, ACT.Copy).then_inc(s_gev_a, 1)
                            if held_after(g + 1) is not None:
                                x_hi(act, EARLY + held_after(g + 1) + XR - 1)
                        for m in range(EARLY, NKEY):
                            if m >= EARLY + HELD:
                                x_hi(act, m + XR - 1)
                            if m % 2:
                                if m >= EARLY + 4:
                                    act.wait_ge(s_gated, (m - EARLY) // 2 - 1)
                                activations(m, gelu[:, (m - EARLY) // 2 % 2])

                        def p_hi_pair(r):
                            if r < NKEY // 2:
                                if r >= 2:
                                    act.wait_ge(s_xu, VU + 2 * (r - 2) + 2)
                                else:
                                    act.wait_ge(s_gated, LATE_PAIRS - 1 + r)
                                A.activation(p_hi[:, pslot(r)], acts[:, 2 * r:2 * r + 2, :], ACT.Copy).then_inc(s_phi, 1)

                        act.wait_ge(s_gev_v, GT)
                        act.wait_ge(s_gev_a, GT)
                        p_hi_pair(0)
                        for i in range(NKEY):
                            if i % 2 == 0:
                                p_hi_pair(i // 2 + 1)
                            x_hi(act, VU + i + XR - 1)

                    @block.gpsimd
                    def _(pool):
                        for m in range(XR - 1, EARLY + XR - 1):
                            x_lo(pool, m)
                        pool.wait_ge(s_gttk, NT)
                        for g in range(GT):
                            pool.wait_ge(s_hot, g + 1)
                            h1, n = hots(g)[:, 0, 0:GB - 1, :], GB - 1
                            PO.tensor_tensor(h1, h1, over(choice[:, 2, GB * g:GB * g + n], P), ALU.mult).then_inc(s_wp, 1)
                            if held_after(g) is not None:
                                x_lo(pool, EARLY + held_after(g) + XR - 1)
                        for m in range(EARLY + HELD + XR - 1, NKEY):
                            x_lo(pool, m)

                    @block.vector
                    def _(dve):
                        def key_top(t, hx):
                            s = s_key[:, t, hx, :]
                            c = cut[:, 0:P]
                            dch.link(V.max(top_v[:, hx, 0:8], s))
                            dch.add(V.max_index(top_iu[:, hx, 0:8], top_v[:, hx, 0:8], s))
                            dch.link(V.match_replace(c, top_v[:, hx, 0:8], s, -3e38))
                            dch.link(V.max(top_v[:, hx, 8:16], c))
                            dch.add(V.max_index(top_iu[:, hx, 8:16], top_v[:, hx, 8:16], c))

                        def candidates():
                            dch.settle()
                            dch.add(V.tensor_copy(top_i[:], top_iu[:]))
                            tv = top_v[:].rearrange("p (h x) k -> p h x k", x=2)
                            for h in range(PH):
                                dch.add(V.tensor_tensor(cand[:, h, :].rearrange("p (a b) -> p a b", a=TOPK),
                                                        over(tv[:, h, 0, :], TOPK), times(tv[:, h, 1, :], TOPK), ALU.add))
                            dch.settle()

                        def pair_top(h):
                            s = cand[:, h, :]
                            dch.link(V.max(best[:, h, 0:8], s))
                            dch.add(V.max_index(pos[:, h, 0:8], best[:, h, 0:8], s))
                            dch.link(V.match_replace(cut[:], best[:, h, 0:8], s, -3e38))
                            dch.link(V.max(best[:, h, 8:16], cut[:]))
                            dch.add(V.max_index(pos[:, h, 8:16], best[:, h, 8:16], cut[:]))

                        def chosen(t):
                            dch.settle()
                            V.tensor_tensor(gate_rows(t), best[:], over(best[:, :, 0], TOPK), ALU.subtract).then_inc(s_cand, 1)
                            pf = pos[:].rearrange("p h k -> p (h k)")
                            ti = top_i[:].rearrange("p (h x) k -> p h x k", x=2)
                            for half in range(2):
                                dch.link(V.tensor_scalar(part[:], pf, (4, 15)[half], None,
                                                         (ALU.logical_shift_right, ALU.bitwise_and)[half]))
                                dch.link(V.tensor_copy(partf[:], part[:]))
                                dch.link(V.tensor_tensor(place[:], over(partf[:], 16), times(cst[:, C_IOTA:C_IOTA + 16], STEPS),
                                                         ALU.is_equal))
                                for h in range(PH):
                                    hh = place[:, h * TOPK:(h + 1) * TOPK, :]
                                    dch.add(V.tensor_tensor(hh, hh, times(ti[:, h, half, :], TOPK), ALU.mult))
                                dch.settle()
                                dch.link(V.tensor_reduce(sel[:, t, half, :], place[:], AX, ALU.add))

                        for t in range(NT):
                            for hx in range(16):
                                key_top(t, hx)
                            candidates()
                            for h in range(PH):
                                pair_top(h)
                            chosen(t)
                        dve.sem_inc(s_cand, 1)
                        for t in range(NT):
                            dve.wait_ge(s_gexp, t + 1)
                            dch.link(V.tensor_reduce(gs[:, t, 0, :], gate_rows(t), AX, ALU.add))
                            dch.link(V.reciprocal(gs[:, t, 1, :], gs[:, t, 0, :]))
                            dch.link(V.tensor_tensor(gate_rows(t), gate_rows(t), over(gs[:, t, 1, :], TOPK), ALU.mult))
                        dve.sem_inc(s_chosen, 1)
                        for t in range(NT):
                            dve.wait_ge(s_gt, t + 1)
                            V.tensor_copy(choice[:, :, t * P:(t + 1) * P],
                                          bank[t][:, 0:3 * P].rearrange("p (j s) -> p j s", j=3)).then_inc(s_gttk, 1)
                        dve.wait_ge(s_gttk, NT)

                        def gated(r):
                            dve.wait_ge(s_uev, EARLY // 2 + r + 1)
                            a = acts[:, EARLY + 2 * r:EARLY + 2 * r + 2, :]
                            V.tensor_tensor(a, a, gelu[:, r % 2], ALU.mult).then_inc(s_gated, 1)

                        for g in range(GT + LAG):
                            if g == LAG:
                                dve.wait_ge(s_uev, EARLY // 2)
                            if g < GT:
                                if g >= 3:
                                    dve.wait_ge(s_gates, g - 2)
                                V.tensor_tensor(hots(g), cst[:, C_IOTA:C_IOTA + NKEY].unsqueeze(1).unsqueeze(1).to_broadcast([P, 2, GB, NKEY]),
                                                choice[:, 0:2, GB * g:GB * (g + 1)].unsqueeze(3).to_broadcast([P, 2, GB, NKEY]),
                                                ALU.is_equal).then_inc(s_hot, 1)
                            if g >= LAG:
                                dve.wait_ge(s_gates, g - LAG + 1)
                                a, b = spread(g - LAG, slice(0, EARLY))
                                V.tensor_tensor(a, a, b, ALU.mult).then_inc(s_gev_v, 1)
                        dve.wait_ge(s_gev_a, GT)
                        def p_lo_pair(r):
                            if r < NKEY // 2:
                                dve.wait_ge(s_phi, r + 1)
                                i = 2 * r % QUARTER
                                V.tensor_tensor(acts_lo[2 * r // QUARTER][:, i:i + 2, :], acts[:, 2 * r:2 * r + 2, :],
                                                p_hi[:, pslot(r)].bitcast(F32), ALU.subtract).then_inc(s_plo, 1)

                        for r in range(LATE_PAIRS - 1):
                            gated(r)
                        dve.wait_ge(s_gev_v, GT)
                        p_lo_pair(0)
                        for i in range(XR - 2):
                            x_lo(dve, VU + i)
                        gated(LATE_PAIRS - 1)
                        x_lo(dve, VU + XR - 2)
                        dve.wait_ge(s_gated, LATE_PAIRS)
                        for i in range(NKEY):
                            if i % 2 == 0:
                                p_lo_pair(i // 2 + 1)
                            if i + XR - 1 < NKEY:
                                x_lo(dve, VU + i + XR - 1)
                        dve.wait_ge(s_xu, 2 * NKEY)
                        for t in range(NT):
                            for h in range(2):
                                xv = x[:, t, h * 512:(h + 1) * 512]
                                V.tensor_tensor(xv, xv, bank[2 * t + h][:], ALU.add).then_inc(s_xffn, 1)
                        dve.wait_ge(s_xffn, 4)

            clear()

        with nc.Block(no_gpsimd_drain=True) as block:
            @block.sync
            def _(sp):
                sp.dma_start(out.rearrange("(t p) d -> p t d", p=P), x[:]).then_inc(s_store, 16)
                sp.wait_ge(s_store, 16)


def _tiles(w):
    k, n = w.shape
    return w.reshape(k // P, P, n).transpose(1, 0, 2).reshape(P, -1)


def _vectors(v):
    return v.reshape(-1, P).T


def _layout(a):
    heads = [g * NP + i for i in range(NP) for g in range(G)]
    q_cols = np.concatenate([np.arange(h * DH, (h + 1) * DH) for h in heads])
    gate_cols = np.concatenate([np.arange(3 * h, 3 * h + 3) for h in heads])
    kv = 1024 + np.arange(768).reshape(6, 128)
    ag = 1792 + gate_cols
    lx, lg, z = 1840, 2864, 3888
    xbc, dt, mg = 4912, 6448, 6464
    stream = np.zeros((L, PIECES, P, WCOL), np.float32)
    small = np.zeros((L, P, SMALL), np.float32)
    rows = np.zeros((L, ROWS), np.float32)
    for l in range(L):
        w = a["w_in"][l]

        def put(g, cols):
            for h in range(2):
                c = cols[:, 256 * h:256 * (h + 1)]
                stream[l, 2 * g + h].reshape(P, KT, 256)[:, :, 0:c.shape[1]] = _tiles(c).reshape(P, KT, -1)

        put(KV0, w[:, np.concatenate([kv[0], kv[2], kv[4], kv[1]])])
        put(KV1, w[:, np.concatenate([kv[3], kv[5], ag, dt + np.arange(SH)])])
        for g in range(2):
            put(Q0 + g, w[:, q_cols[512 * g:512 * (g + 1)]])
            put(LX0 + g, w[:, lx + 512 * g:lx + 512 * (g + 1)])
            put(LG0 + g, w[:, lg + 512 * g:lg + 512 * (g + 1)])
            put(Z0 + g, w[:, z + 512 * g:z + 512 * (g + 1)])
            put(OUT0 + g, a["w_out"][l][:, 512 * g:512 * (g + 1)])
            stream[l, 2 * W1K + g] = _tiles(a["cmp_k_w1"][l][1024 * g:1024 * (g + 1)])
            stream[l, 2 * W1V + g] = _tiles(a["cmp_v_w1"][l][1024 * g:1024 * (g + 1)])
        for g in range(3):
            put(XBC0 + g, w[:, xbc + 512 * g:xbc + 512 * (g + 1)])
        for g in range(6):
            put(MG0 + g, w[:, mg + 512 * g:mg + 512 * (g + 1)])
            wb = a["w_branch"][l, g // 2]
            if g < 2:
                wb = wb[q_cols]
            put(BR0 + g, wb[:, 512 * (g % 2):512 * (g % 2 + 1)])
        for g in range(4):
            put(PQ0 + g, a["peer_w_q"][l][:, 512 * g:512 * (g + 1)])

        parts = {
            "mix_g": _vectors(a["mix_norm_g"][l]), "conv_w": _vectors(a["lru_conv_w"][l]),
            "conv_b": _vectors(a["lru_conv_b"][l]), "b_r": _vectors(a["lru_b_r"][l]),
            "b_i": _vectors(a["lru_b_i"][l]), "lam": _vectors(a["lru_lambda"][l]),
            "xconv_w": _vectors(a["ssm_conv_w"][l]), "xconv_b": _vectors(a["ssm_conv_b"][l]),
            "ssm_g": _vectors(a["ssm_norm_g"][l]),
            "pe": np.concatenate([_vectors(a["cmp_pe_k"][l]), _vectors(a["cmp_pe_v"][l])], 1),
        }
        for name, v in parts.items():
            small[l, :, _vec[name][0]:_vec[name][1]] = v
        wl = np.zeros((P, 2, KT, P), np.float32)
        for j, name in enumerate(("lru_w_r", "lru_w_i")):
            for h in range(16):
                o = (h % 2) * 64
                wl[o:o + 64, j, h // 2, o:o + 64] = a[name][l, h]
        small[l, :, VEC:VEC + LRU_W] = wl.reshape(P, -1)
        small[l, :, VEC + LRU_W:] = np.concatenate([_tiles(a["cmp_k_w2"][l]), _tiles(a["cmp_v_w2"][l])], 1)
        rows[l] = np.concatenate([a["ssm_dt_bias"][l], a["ssm_a_log"][l], a["ssm_d"][l], a["q_norm_g"][l], a["k_norm_g"][l]])
    sk = a["peer_sub_keys"].transpose(0, 4, 1, 2, 3).reshape(L, P, 16, P)
    xs = np.empty((L, 2 * NKEY, P, D), np.float32)
    xs[:, :NKEY] = a["peer_u"].reshape(L, NKEY, NKEY, KT, P).transpose(0, 2, 4, 3, 1).reshape(L, NKEY, P, D)
    xs[:, NKEY:] = a["peer_v"].reshape(L, NKEY, NKEY, D).transpose(0, 2, 1, 3)
    return {
        "x": a["x"].reshape(S, D), "pos_tok": a["positions"].reshape(NT, P).T, "pos_row": a["positions"].reshape(S),
        "const": constants(), "wstream": stream.reshape(L * PIECES, P, WCOL), "small": small, "rows": rows,
        "ffn_row": a["ffn_norm_g"], "subkeys": sk, "xstream": xs.reshape(L * 2 * NKEY, P, D),
    }


def kernel(**inputs):
    import concourse.bacc as bacc
    from concourse.bass_utils import run_bass_kernel_spmd

    nc = bacc.Bacc("TRN2", target_bir_lowering=False, num_devices=1)
    arrays, args = {}, []
    for name, a in _layout({k: np.asarray(v) for k, v in inputs.items()}).items():
        a = np.ascontiguousarray(a)
        arrays[f"in_{name}"] = a
        args.append(nc.dram_tensor(f"in_{name}", a.shape, mybir.dt.from_np(a.dtype), kind="ExternalInput").ap())
    o = nc.dram_tensor("out_0", (S, D), F32, kind="ExternalOutput").ap()
    trunk(nc, *args, o)
    r = run_bass_kernel_spmd(nc, [arrays], core_ids=[0])
    return r.results[0]["out_0"].reshape(1, S, D)
```
